# Optimizing a Trainium2 kernel written in Bass

```python
import jax, jax.numpy as jnp
from jax import lax
import numpy as np

D_MODEL = 1024
BATCH = 1
SEQ = 1024
DEPTH = 1

D_RNN = D_MODEL
RNN_HEADS = 8
RNN_HEAD_DIM = D_RNN // RNN_HEADS
CONV_WIDTH = 4
LRU_C = 8.0
D_GMLP = D_MODEL
GMLP_HEADS = 8
GMLP_HEAD_DIM = D_GMLP // GMLP_HEADS
CHUNK = 128
N_BRANCH = 2
D_IN = 2 * D_RNN + 2 * D_GMLP + N_BRANCH * D_MODEL
PEER_HEADS = 8
N_KEYS = 128
N_EXPERTS = N_KEYS * N_KEYS
D_KEY = 256
D_HALF = D_KEY // 2
TOPK = 16
TOK_BLOCK = 128
ALPHA = (2.0 * DEPTH) ** 0.25
BETA = (8.0 * DEPTH) ** -0.25
LN_EPS = 1e-5

kernel_name = "hybrid_rglru_gmlp_peer_deepnorm"

def layer_norm(x, g, b):
    xf = x.astype(jnp.float32)
    mu = jnp.mean(xf, axis=-1, keepdims=True)
    var = jnp.mean(jnp.square(xf - mu), axis=-1, keepdims=True)
    y = (xf - mu) * lax.rsqrt(var + LN_EPS) * g.astype(jnp.float32) + b.astype(jnp.float32)
    return y.astype(x.dtype)

def causal_depthwise_conv(x, w, b):
    s = x.shape[1]
    xp = jnp.pad(x, ((0, 0), (CONV_WIDTH - 1, 0), (0, 0)))
    return sum(w[k] * xp[:, k:k + s] for k in range(CONV_WIDTH)) + b

def rg_lru(x, w_a, b_a, w_x, b_x, lam):
    bsz, s, _ = x.shape
    xh = x.reshape(bsz, s, RNN_HEADS, RNN_HEAD_DIM)
    r = jax.nn.sigmoid(jnp.einsum('bshi,hij->bshj', xh, w_a).reshape(bsz, s, D_RNN) + b_a)
    i = jax.nn.sigmoid(jnp.einsum('bshi,hij->bshj', xh, w_x).reshape(bsz, s, D_RNN) + b_x)
    log_a = -LRU_C * r.astype(jnp.float32) * jax.nn.softplus(-lam.astype(jnp.float32))
    a = jnp.exp(log_a)
    mult = jnp.sqrt(-jnp.expm1(2.0 * log_a))
    bx = mult * (i * x).astype(jnp.float32)

    def combine(e1, e2):
        a1, b1 = e1
        a2, b2 = e2
        return a1 * a2, a2 * b1 + b2

    _, h = lax.associative_scan(combine, (a, bx), axis=1)
    return h.astype(x.dtype)

def chunked_spatial_gating(u, v, ln_g, ln_b, ws, bs):
    bsz, s, _ = u.shape
    u = jax.nn.gelu(u)
    v = layer_norm(jax.nn.gelu(v), ln_g, ln_b)
    vc = v.reshape(bsz, s // CHUNK, CHUNK, GMLP_HEADS, GMLP_HEAD_DIM)
    mask = jnp.tril(jnp.ones((CHUNK, CHUNK), dtype=bool))
    wsm = jnp.where(mask[None], ws, jnp.zeros_like(ws))
    mixed = jnp.einsum('hts,bcshd->bcthd', wsm, vc) + bs.T[None, None, :, :, None]
    return u * mixed.reshape(bsz, s, D_GMLP)

def peer(x, wq, sub_keys, u_tab, v_tab):
    bsz, s, d = x.shape
    t = bsz * s
    xt = x.reshape(t, d)
    q = (xt @ wq).reshape(t, PEER_HEADS, 2, D_HALF).astype(jnp.float32)
    scores = jnp.einsum('thpd,hpnd->thpn', q, sub_keys.astype(jnp.float32))
    s1, i1 = lax.top_k(scores[:, :, 0], TOPK)
    s2, i2 = lax.top_k(scores[:, :, 1], TOPK)
    cand_s = (s1[..., :, None] + s2[..., None, :]).reshape(t, PEER_HEADS, TOPK * TOPK)
    cand_i = (i1[..., :, None] * N_KEYS + i2[..., None, :]).reshape(t, PEER_HEADS, TOPK * TOPK)
    top_s, pos = lax.top_k(cand_s, TOPK)
    idx = jnp.take_along_axis(cand_i, pos, axis=-1)
    gate = jax.nn.softmax(top_s, axis=-1).astype(x.dtype)
    nb = t // TOK_BLOCK

    def block(args):
        xb, ib, gb = args
        u_sel = u_tab[ib]
        h = jnp.einsum('thkd,td->thk', u_sel, xb)
        act = jax.nn.gelu(h) * gb
        return jnp.einsum('thk,thkd->td', act, v_tab[ib])

    out = lax.map(block, (xt.reshape(nb, TOK_BLOCK, d),
                          idx.reshape(nb, TOK_BLOCK, PEER_HEADS, TOPK),
                          gate.reshape(nb, TOK_BLOCK, PEER_HEADS, TOPK)))
    return out.reshape(bsz, s, d)

def setup_inputs(seed: int = 0) -> dict:
    key = jax.random.key(seed)
    ks = jax.random.split(key, 24)
    nrm = lambda k, shape, scale: jax.random.normal(k, shape, jnp.float32) * scale
    L = DEPTH
    a0 = jax.random.uniform(ks[9], (L, D_RNN), jnp.float32, minval=0.9, maxval=0.999)
    return {
        "x": nrm(ks[0], (BATCH, SEQ, D_MODEL), 1.0),
        "w_in": nrm(ks[1], (L, D_MODEL, D_IN), D_MODEL ** -0.5),
        "b_gate": nrm(ks[2], (L, N_BRANCH, D_MODEL), 0.02),
        "conv_w": nrm(ks[3], (L, CONV_WIDTH, D_RNN), CONV_WIDTH ** -0.5),
        "conv_b": nrm(ks[4], (L, D_RNN), 0.02),
        "rg_w_a": nrm(ks[5], (L, RNN_HEADS, RNN_HEAD_DIM, RNN_HEAD_DIM), RNN_HEAD_DIM ** -0.5),
        "rg_b_a": nrm(ks[6], (L, D_RNN), 0.02),
        "rg_w_x": nrm(ks[7], (L, RNN_HEADS, RNN_HEAD_DIM, RNN_HEAD_DIM), RNN_HEAD_DIM ** -0.5),
        "rg_b_x": nrm(ks[8], (L, D_RNN), 0.02),
        "rg_lambda": jnp.log(a0) - jnp.log1p(-a0),
        "gm_ln_g": 1.0 + nrm(ks[10], (L, D_GMLP), 0.02),
        "gm_ln_b": nrm(ks[11], (L, D_GMLP), 0.02),
        "gm_ws": nrm(ks[12], (L, GMLP_HEADS, CHUNK, CHUNK), CHUNK ** -0.5),
        "gm_bs": 1.0 + nrm(ks[13], (L, GMLP_HEADS, CHUNK), 0.02),
        "w_out": nrm(ks[14], (L, D_MODEL, D_MODEL), BETA * D_MODEL ** -0.5),
        "ln1_g": 1.0 + nrm(ks[15], (L, D_MODEL), 0.02),
        "ln1_b": nrm(ks[16], (L, D_MODEL), 0.02),
        "peer_wq": nrm(ks[17], (L, D_MODEL, PEER_HEADS * D_KEY), D_MODEL ** -0.5),
        "peer_sub_keys": nrm(ks[18], (L, PEER_HEADS, 2, N_KEYS, D_HALF), D_HALF ** -0.5),
        "peer_u": nrm(ks[19], (L, N_EXPERTS, D_MODEL), D_MODEL ** -0.5),
        "peer_v": nrm(ks[20], (L, N_EXPERTS, D_MODEL), BETA),
        "ln2_g": 1.0 + nrm(ks[21], (L, D_MODEL), 0.02),
        "ln2_b": nrm(ks[22], (L, D_MODEL), 0.02),
    }

def reference(x, w_in, b_gate, conv_w, conv_b, rg_w_a, rg_b_a, rg_w_x, rg_b_x, rg_lambda,
              gm_ln_g, gm_ln_b, gm_ws, gm_bs, w_out, ln1_g, ln1_b,
              peer_wq, peer_sub_keys, peer_u, peer_v, ln2_g, ln2_b):
    bsz, s, _ = x.shape
    splits = [D_RNN, 2 * D_RNN, 2 * D_RNN + D_GMLP, 2 * D_RNN + 2 * D_GMLP]
    for l in range(DEPTH):
        proj = x @ w_in[l]
        xa, ga, u, v, g = jnp.split(proj, splits, axis=-1)
        ya = jax.nn.gelu(ga) * rg_lru(causal_depthwise_conv(xa, conv_w[l], conv_b[l]),
                                      rg_w_a[l], rg_b_a[l], rg_w_x[l], rg_b_x[l], rg_lambda[l])
        yb = chunked_spatial_gating(u, v, gm_ln_g[l], gm_ln_b[l], gm_ws[l], gm_bs[l])
        gates = jax.nn.sigmoid(g.reshape(bsz, s, N_BRANCH, D_MODEL) + b_gate[l])
        y = gates[:, :, 0] * ya + gates[:, :, 1] * yb
        x = layer_norm(ALPHA * x + y @ w_out[l], ln1_g[l], ln1_b[l])
        x = layer_norm(ALPHA * x + peer(x, peer_wq[l], peer_sub_keys[l], peer_u[l], peer_v[l]),
                       ln2_g[l], ln2_b[l])
    return x


_drawn_inputs = setup_inputs


def setup_inputs(seed=0):
    import zlib

    import numpy as np

    out = dict(_drawn_inputs(seed))
    spreads = {}
    factors = {'b_gate': 4.763,
     'rg_b_a': 29.872,
     'rg_b_x': 25.474,
     'gm_ln_g': 4.167,
     'gm_ln_b': 4.191,
     'gm_bs': 3.511,
     'ln2_g': 7.53,
     'ln2_b': 7.755}
    for name, (base, spread) in spreads.items():
        noise = np.random.default_rng([zlib.crc32(name.encode()), seed]).standard_normal(out[name].shape)
        drawn = base * np.exp(spread * noise) if base else spread * noise
        out[name] = __import__('jax').numpy.asarray(drawn.astype(out[name].dtype))
    for name, factor in factors.items():
        out[name] = (out[name] * factor).astype(out[name].dtype)
    return out
```

```python
from contextlib import ExitStack

import concourse.bass as bass
from concourse import mybir

ALU = mybir.AluOpType
ACT = mybir.ActivationFunctionType
F32 = mybir.dt.float32
U32 = mybir.dt.uint32
U16 = mybir.dt.uint16
AX_X = mybir.AxisListType.X

P = 128
D = 1024
T = 1024
KT = D // P
CT = D // P
HALF = 512
NHALF = T // HALF
BPH = HALF // P
NBLK = T // P
HEADS = 8
NKEY = 128
TOPK = 16
QT = 2 * HEADS
NG = NBLK * HEADS
RING = 8
LEAD = 3
CONV = 4
LRU_C = 8.0
ALPHA = 2.0 ** 0.25
EPS = 1e-5
LOWEST = -3.0e38
TILE = KT * P
MIXW = 5 * TILE + 2 * P
CW, CB, BA, BX, LAM, BGA, BGB = 0, 4, 5, 6, 7, 8, 9
NCHAN = 10
XA, GA, R, I, U, MIX, G_A, G_B = range(8)


def build(nc, x, x_t, w_mix, w_v, w_out, w_q, keys_t, ws_t, bs, chan_d, ln_d, peer_u, peer_v, out):
    with ExitStack() as ctx:
        def sb(name, shape, dt=F32):
            return ctx.enter_context(nc.sbuf_tensor(name, shape, dt))

        def sem(name):
            return ctx.enter_context(nc.semaphore(name))

        arena = sb("arena", [P, 2 * MIXW + 3 * KT * HALF])
        w_buf = [arena[:, i * MIXW:(i + 1) * MIXW] for i in range(2)]
        o = 2 * MIXW
        xt = arena[:, o:o + KT * HALF].rearrange("p (k t) -> p k t", k=KT)
        o += KT * HALF
        v_area = arena[:, o:o + KT * HALF]
        v_tok = v_area.rearrange("p (b c) -> p b c", b=BPH)
        x1t = v_area.rearrange("p (k t) -> p k t", k=KT)
        o += KT * HALF
        y_t = arena[:, o:o + KT * HALF].rearrange("p (c t) -> p c t", c=CT)
        u_ring = [arena[:, s * D:(s + 1) * D] for s in range(RING)]
        v_ring = [arena[:, 2 * MIXW + s * D:2 * MIXW + (s + 1) * D] for s in range(RING)]
        diag = arena[:, o:o + RING * P].rearrange("p (s t) -> p s t", s=RING)
        x1_now = arena[:, o + D:o + 2 * D]
        res = arena[:, o + 2 * D:o + 3 * D]

        x1 = sb("x1", [P, NBLK, D])
        keys = sb("keys", [P, QT, NKEY])
        ws = sb("ws", [P, CT, P])
        bs_b = sb("bs_b", [P, CT, P])
        ln_gb = sb("ln_gb", [P, 2, D])
        chan = sb("chan", [P, NCHAN, CT])
        xa = sb("xa", [P, CONV - 1 + HALF])
        halo = sb("halo", [P, CT, CONV - 1])
        h_last = sb("h_last", [P, CT])
        xc, gg, rr, ii, aa, a2, gu, s_a, s_b = (
            sb(n, [P, HALF]) for n in ("xc", "gg", "rr", "ii", "aa", "a2", "gu", "s_a", "s_b"))
        v_st = sb("v_st", [P, BPH, P])
        q_s = sb("q_s", [P, 2, HALF])
        knock = sb("knock", [P, BPH, NKEY])
        top_st = sb("top_st", [P, BPH, HEADS, TOPK])
        key_st = sb("key_st", [P, BPH, HEADS, TOPK], U16)
        top_v = sb("top_v", [P, NG, 2, TOPK])
        top_i = sb("top_i", [P, NG, 2, TOPK], U16)
        ids = sb("ids", [P, NG, TOPK], U32)
        gates = sb("gates", [P, NG * TOPK])
        id_now = sb("id_now", [P, 2, TOPK], U32)
        cand = sb("cand", [P, TOPK * TOPK])
        cand2 = sb("cand2", [P, TOPK * TOPK])
        best = sb("best", [P, TOPK])
        pos = sb("pos", [P, TOPK], U32)
        pair = sb("pair", [P, 2, TOPK], U32)
        hot = sb("hot", [P, 2, TOPK, TOPK])
        picked = sb("picked", [P, 2, TOPK])
        less = sb("less", [P, TOPK])
        expo = sb("expo", [P, TOPK])
        tot = sb("tot", [P, 2])
        hdot = sb("hdot", [P, 2, RING])
        hact = sb("hact", [P, 2, RING])
        wact = sb("wact", [P, RING])
        ident = sb("ident", [P, P])
        ident_a = sb("ident_a", [P, P])
        iota = sb("iota", [P, TOPK], U32)
        stats = sb("stats", [P, BPH, 2, 6])
        mv = sb("mv", [P, BPH, 2])
        rstd = sb("rstd", [P, BPH])
        sp = sb("sp", [P, 6, CT])
        dec = sb("dec", [P, 2, CT])
        ps = ctx.enter_context(nc.psum_tensor("ps", [P, 8, HALF], F32))

        const_in, xt_in, x_in, ln_in = sem("const_in"), sem("xt_in"), sem("x_in"), sem("ln_in")
        w_in = [sem("w_in0"), sem("w_in1")]
        masks = sem("masks")
        lam_abs, lam_exp, dec_ready = sem("lam_abs"), sem("lam_exp"), sem("dec_ready")
        v_mm, v_gelu, v_norm = sem("v_mm"), sem("v_gelu"), sem("v_norm")
        xa_mm, ga_mm, ri_mm, u_mm, mix_mm, g_a_mm, g_b_mm = (
            sem(n) for n in ("xa_mm", "ga_mm", "ri_mm", "u_mm", "mix_mm", "g_a_mm", "g_b_mm"))
        xa_ev, ga_ev, ri_ev, u_ev, mix_ev, g_a_ev, g_b_ev = (
            sem(n) for n in ("xa_ev", "ga_ev", "ri_ev", "u_ev", "mix_ev", "g_a_ev", "g_b_ev"))
        xc_ready, decay = sem("xc_ready"), sem("decay")
        one_less, root = sem("one_less"), sem("root")
        var_ready, std_ready = sem("var_ready"), sem("std_ready")
        y_done = sem("y_done")
        st_ready = sem("st_ready")
        o_mm, o_ev, x1_ready, t_mm, t_ev = (
            sem(n) for n in ("o_mm", "o_ev", "x1_ready", "t_mm", "t_ev"))
        q_mm, sc_mm = sem("q_mm"), sem("sc_mm")
        q_ev, sc_ev = sem("q_ev"), sem("sc_ev")
        ids_ready, less_ready, exp_done = sem("ids_ready"), sem("less_ready"), sem("exp_done")
        id_copied = sem("id_copied")
        u_in = [sem(f"u_in{s}") for s in range(RING)]
        v_in = [sem(f"v_in{s}") for s in range(RING)]
        u_used, v_used = sem("u_used"), sem("v_used")
        gelu_done, diag_ready = sem("gelu_done"), sem("diag_ready")
        out_ev = sem("out_ev")
        fin = sem("fin")
        res_free = sem("res_free")
        stored = sem("stored")
        tick = sem("tick")

        def wait_alone(eng, s, value):
            eng.wait_ge(s, value)
            eng.sem_inc(tick, 1)

        def wtile(buf, j):
            return buf[:, j * TILE:(j + 1) * TILE].rearrange("p (k c) -> p k c", k=KT)

        def whalf(buf):
            return buf[:, 0:KT * HALF].rearrange("p (k c) -> p k c", k=KT)

        block = ctx.enter_context(nc.Block())

        @block.sync
        def _(eng):
            eng.sem_inc(res_free, 1)

            def load_ln(n):
                for j in range(2):
                    eng.dma_start(ln_gb[:, j, :], ln_d[n, j].partition_broadcast(P)).then_inc(ln_in, 16)

            for h in range(NHALF):
                if h:
                    eng.wait_ge(g_b_mm, CT * h)
                eng.dma_start(xt, x_t[h].rearrange("p (k t) -> p k t", k=KT)).then_inc(xt_in, 16)
                for j in range(2):
                    if h:
                        eng.wait_ge(q_mm, QT * h - 4 + 4 * j)
                    eng.dma_start(w_buf[j][:, 0:KT * HALF], w_v[j]).then_inc(w_in[j], 16)
                if h == 0:
                    eng.dma_start(chan[:, :, :], chan_d).then_inc(const_in, 16)
                    eng.dma_start(keys[:, :, :], keys_t).then_inc(const_in, 16)
                    eng.dma_start(ws[:, :, :], ws_t).then_inc(const_in, 16)
                    eng.dma_start(bs_b[:, :, :].rearrange("p c t -> p (c t)"),
                                  bs.partition_broadcast(P)).then_inc(const_in, 16)
                    load_ln(0)
                eng.dma_start(x1[:, h * BPH:(h + 1) * BPH, :],
                              x[h * HALF:(h + 1) * HALF, :].rearrange("(b p) d -> p b d", p=P)
                              ).then_inc(x_in, 16)
                for j in range(2):
                    eng.wait_ge(v_mm, 2 * BPH * h + BPH * (j + 1))
                    eng.dma_start(w_buf[j], w_mix[j]).then_inc(w_in[j], 16)
                with eng.Fori(1, CT // 2) as cc:
                    for j in range(2):
                        eng.wait_ge(g_b_mm, 2 * cc + (CT * h + j - 1))
                        eng.dma_start(w_buf[j], w_mix[bass.ds(2 * cc + j, 1)].rearrange(
                            "a p n -> (a p) n")).then_inc(w_in[j], 16)
                eng.wait_ge(v_norm, h + 1)
                load_ln(1)
                for j in range(2):
                    eng.wait_ge(g_b_mm, CT * h + CT - 1 + j)
                    eng.dma_start(w_buf[j][:, 0:KT * HALF], w_out[j]).then_inc(w_in[j], 16)
                for j in range(4):
                    if j < 2:
                        eng.wait_ge(o_mm, 2 * BPH * h + BPH * (j + 1))
                    else:
                        eng.wait_ge(q_mm, QT * h + 4 * (j - 1))
                    eng.dma_start(w_buf[j % 2][:, 0:4 * TILE], w_q[j]).then_inc(w_in[j % 2], 16)
                eng.wait_ge(x1_ready, BPH * (h + 1))
                load_ln(0 if h < NHALF - 1 else 2)
            with eng.Fori(0, NBLK) as b:
                wait_alone(eng, fin, b + 1)
                eng.dma_start(out[bass.ds(b * P, P), :], res).then_inc(stored, 16)
                wait_alone(eng, stored, 16 * b + 16)
                eng.sem_inc(res_free, 1)

        @block.gpsimd
        def _(eng):
            eng.memset(ident[:, :], 0.0)
            eng.iota(iota[:, :], pattern=[[1, TOPK]], base=0, channel_multiplier=0)
            eng.drain()
            eng.affine_select(out=ident[:, :], in_=ident[:, :], compare_op=ALU.not_equal, fill=1.0,
                              base=0, pattern=[[-1, P]], channel_multiplier=1)
            eng.wait_ge(const_in, 64)
            eng.affine_select(out=ws[:, :, :], in_=ws[:, :, :], compare_op=ALU.is_ge, fill=0.0,
                              base=0, pattern=[[0, CT], [1, P]], channel_multiplier=-1
                              ).then_inc(masks, 1)

            for h in range(NHALF):
                eng.wait_ge(v_norm, h + 1)
                with eng.Fori(0, CT) as c:
                    wait_alone(eng, mix_mm, c + (CT * h + 1))
                    eng.tensor_copy(v_st[:, :, :], v_tok[:, :, bass.ds(c * P, P)]).then_inc(st_ready, 1)

            def gather(ring, landed, table, used, par, g, c, s):
                wait_alone(eng, used, g * (2 * RING) + (c * RING + s + 1))
                eng.indirect_dma_start(ring[s], None, table, bass.IndirectOffsetOnAxis(
                    ap=id_now[:, par, c * RING + s:c * RING + s + 1], axis=0)).then_inc(landed[s], 16)

            def gather_u(par, g, c):
                for s in range(RING):
                    gather(u_ring, u_in, peer_u, u_used, par, g, c, s)

            def gather_v(par, g, c):
                for s in range(RING):
                    gather(v_ring, v_in, peer_v, v_used, par, g, c, s)

            def head(par, g, first=False):
                wait_alone(eng, ids_ready, g + 1)
                eng.tensor_copy(id_now[:, par, :], ids[:, bass.ds(g, 1), :].rearrange(
                    "p a k -> p (a k)")).then_inc(id_copied, 1)
                eng.drain()
                gather_u(par, g, 0)
                if not first:
                    gather_v(1 - par, g - 1, 1)
                gather_u(par, g, 1)
                gather_v(par, g, 0)

            eng.wait_ge(q_mm, QT * NHALF)
            head(0, 0, first=True)
            head(1, 1)
            with eng.Fori(1, NG // 2) as gg2:
                head(0, gg2 * 2)
                head(1, gg2 * 2 + 1)
            gather_v(1, NG - 1, 1)
            for s in range(RING):
                eng.wait_ge(v_in[s], 16 * 2 * NG)

        @block.scalar
        def _(eng):
            for s in (xa_ev, ga_ev, ri_ev, u_ev, g_a_ev, g_b_ev, out_ev):
                eng.sem_inc(s, 1)
            eng.sem_inc(q_ev, 2)
            eng.wait_ge(lam_abs, 1)
            eng.activation(sp[:, 1, :], sp[:, 0, :], ACT.Exp, scale=-1.0).then_inc(lam_exp, 1)

            def std(lo, hi, n):
                wait_alone(eng, var_ready, n)
                eng.activation(rstd[:, lo:hi], rstd[:, lo:hi], ACT.Sqrt).then_inc(std_ready, 1)

            def tile_a2(h, c):
                n = c + (CT * h + 1)
                ch = lambda row: chan[:, row, bass.ds(c, 1)]
                wait_alone(eng, y_done, n)
                wait_alone(eng, xa_mm, n)
                eng.activation(xa[:, CONV - 1:], ps[:, XA, :], ACT.Copy).then_inc(xa_ev, 1)
                wait_alone(eng, ga_mm, n)
                eng.activation(gg[:, :], ps[:, GA, :], ACT.Gelu_apprx_tanh).then_inc(ga_ev, 1)
                wait_alone(eng, ri_mm, n)
                eng.activation(rr[:, :], ps[:, R, :], ACT.Sigmoid, bias=ch(BA))
                eng.activation(ii[:, :], ps[:, I, :], ACT.Sigmoid, bias=ch(BX)).then_inc(ri_ev, 1)
                eng.drain()
                eng.activation(aa[:, :], rr[:, :], ACT.Exp, scale=dec[:, 0, bass.ds(c, 1)])
                eng.drain()
                eng.activation(rr[:, :], rr[:, :], ACT.Tanh, scale=dec[:, 1, bass.ds(c, 1)])
                eng.activation(a2[:, :], aa[:, :], ACT.Square).then_inc(decay, 1)
                wait_alone(eng, one_less, n)
                eng.activation(rr[:, :], rr[:, :], ACT.Sqrt).then_inc(root, 1)
                wait_alone(eng, u_mm, n)
                eng.activation(gu[:, :], ps[:, U, :], ACT.Gelu_apprx_tanh).then_inc(u_ev, 1)
                wait_alone(eng, g_a_mm, n)
                eng.activation(s_a[:, :], ps[:, G_A, :], ACT.Sigmoid, bias=ch(BGA)).then_inc(g_a_ev, 1)
                wait_alone(eng, g_b_mm, n)
                eng.activation(s_b[:, :], ps[:, G_B, :], ACT.Sigmoid, bias=ch(BGB)).then_inc(g_b_ev, 1)

            for h in range(NHALF):
                for n in range(2 * BPH):
                    eng.wait_ge(v_mm, 2 * BPH * h + n + 1)
                    eng.activation(v_tok[:, n % BPH, (n // BPH) * HALF:(n // BPH + 1) * HALF],
                                   ps[:, 6 + n % 2, :], ACT.Gelu_apprx_tanh).then_inc(v_gelu, 1)
                std(0, BPH, (BPH + 1) * h + 1)
                if h == 0:
                    eng.wait_ge(dec_ready, 1)
                with eng.Fori(0, CT) as c:
                    tile_a2(h, c)
                for b in range(BPH):
                    std(b, b + 1, (BPH + 1) * h + 2 + b)
                for b in range(BPH):
                    for j in range(2):
                        eng.wait_ge(t_mm, 2 * (BPH * h + b) + j + 1)
                        eng.activation(x1t[:, 4 * j:4 * j + 4, b * P:(b + 1) * P],
                                       ps[:, 6 * (1 - b % 2) + j, :].rearrange("p (k t) -> p k t", k=4),
                                       ACT.Copy).then_inc(t_ev, 1)
                with eng.Fori(0, QT // 8) as jj:
                    for i in range(8):
                        n = jj * 8 + (QT * h + i)
                        wait_alone(eng, q_mm, n + 1)
                        wait_alone(eng, sc_ev, n + 1)
                        eng.activation(q_s[:, i % 2, :], ps[:, 2 + i % 2, :], ACT.Copy).then_inc(q_ev, 1)

            def softmax_exp(g):
                wait_alone(eng, less_ready, g + 1)
                eng.activation(expo[:, :], less[:, :], ACT.Exp).then_inc(exp_done, 1)

            def gelu(g, c):
                wait_alone(eng, u_used, g * (2 * RING) + (RING * (c + 1) + RING))
                eng.activation(hact[:, c, :], hdot[:, c, :], ACT.Gelu_apprx_tanh).then_inc(gelu_done, 1)

            def evacuate(b):
                wait_alone(eng, v_used, b * (HEADS * TOPK) + (HEADS * TOPK + RING))
                wait_alone(eng, res_free, b + 1)
                eng.activation(res[:, 0:HALF], ps[:, 0, :], ACT.Copy)
                eng.activation(res[:, HALF:D], ps[:, 1, :], ACT.Copy).then_inc(out_ev, 1)

            def head(g, select=True, evac=None):
                gelu(g, 0)
                if evac is not None:
                    evacuate(evac)
                if select:
                    softmax_exp(g + LEAD)
                gelu(g, 1)
                if evac is not None:
                    std(0, 1, evac + ((BPH + 1) * NHALF + 1))

            with eng.Fori(0, LEAD) as g:
                softmax_exp(g)
            with eng.Fori(0, HEADS) as g:
                head(g)
            with eng.Fori(1, NBLK - 1) as b:
                head(b * HEADS, evac=b - 1)
                with eng.Fori(1, HEADS) as hd:
                    head(b * HEADS + hd)
            last = HEADS * (NBLK - 1)
            head(last, evac=NBLK - 2)
            with eng.Fori(last + 1, NG - LEAD) as g:
                head(g)
            with eng.Fori(NG - LEAD, NG) as g:
                head(g, select=False)
            evacuate(NBLK - 1)
            std(0, 1, NBLK + (BPH + 1) * NHALF)

        @block.tensor
        def _(eng):
            eng.sem_inc(v_used, RING)
            eng.sem_inc(mix_mm, 1)

            def project(bank, w, rhs, done):
                for k in range(KT):
                    mm = eng.matmul(ps[:, bank, :], w[:, k, :], rhs[:, k, :],
                                    start=(k == 0), stop=(k == KT - 1))
                mm.then_inc(done, 1)

            def tile_a2(h, c, par):
                n = c + (CT * h + 1)
                buf = w_buf[par]
                rg = buf[:, 5 * TILE:].rearrange("p (a c) -> p a c", a=2)
                eng.wait_ge(xa_ev, n)
                project(XA, wtile(buf, 0), xt, xa_mm)
                eng.wait_ge(ga_ev, n)
                project(GA, wtile(buf, 1), xt, ga_mm)
                eng.wait_ge(xc_ready, n)
                eng.wait_ge(ri_ev, n)
                eng.matmul(ps[:, R, :], rg[:, 0, :], xc[:, :], start=True, stop=True)
                eng.matmul(ps[:, I, :], rg[:, 1, :], xc[:, :], start=True, stop=True).then_inc(ri_mm, 1)
                eng.wait_ge(u_ev, n)
                project(U, wtile(buf, 2), xt, u_mm)
                eng.wait_ge(g_a_ev, n)
                project(G_A, wtile(buf, 3), xt, g_a_mm)
                eng.wait_ge(st_ready, n)
                eng.wait_ge(mix_ev, n)
                for b in range(BPH):
                    mm = eng.matmul(ps[:, MIX, b * P:(b + 1) * P], v_st[:, b, :],
                                    ws[:, bass.ds(c, 1), :].rearrange("p a t -> p (a t)"),
                                    start=True, stop=True)
                mm.then_inc(mix_mm, 1)
                eng.wait_ge(g_b_ev, n)
                project(G_B, wtile(buf, 4), xt, g_b_mm)

            for h in range(NHALF):
                eng.wait_ge(xt_in, 16 * (h + 1))
                for n in range(2 * BPH):
                    half, b = divmod(n, BPH)
                    if b == 0:
                        eng.wait_ge(w_in[half], 16 * (8 * h + 1))
                    if n >= 2:
                        eng.wait_ge(v_gelu, 2 * BPH * h + n - 1)
                    w = whalf(w_buf[half])
                    for k in range(KT):
                        mm = eng.matmul(ps[:, 6 + n % 2, :], xt[:, k, b * P:(b + 1) * P], w[:, k, :],
                                        start=(k == 0), stop=(k == KT - 1))
                    mm.then_inc(v_mm, 1)
                if h:
                    eng.wait_ge(sc_ev, 2 + QT * h)
                else:
                    eng.wait_ge(masks, 1)
                eng.wait_ge(v_gelu, 2 * BPH * (h + 1))
                with eng.Fori(0, CT // 2) as cc:
                    for par in range(2):
                        eng.wait_ge(w_in[par], cc * 16 + 16 * (8 * h + 2))
                        tile_a2(h, cc * 2 + par, par)
                eng.wait_ge(y_done, CT * (h + 1) + 1)
                for n in range(2 * BPH):
                    half, b = divmod(n, BPH)
                    if b == 0:
                        eng.wait_ge(w_in[half], 16 * (8 * h + 6))
                    if n >= 2:
                        eng.wait_ge(o_ev, 2 * BPH * h + n - 1)
                    w = whalf(w_buf[half])
                    for k in range(CT):
                        mm = eng.matmul(ps[:, 4 + n % 2, :], y_t[:, k, b * P:(b + 1) * P], w[:, k, :],
                                        start=(k == 0), stop=(k == CT - 1))
                    mm.then_inc(o_mm, 1)
                for b in range(BPH):
                    eng.wait_ge(x1_ready, BPH * h + b + 1)
                    if b >= 2:
                        eng.wait_ge(t_ev, 2 * (BPH * h + b - 1))
                    for j in range(2):
                        for k in range(4):
                            mm = eng.transpose(ps[:, 6 * (1 - b % 2) + j, k * P:(k + 1) * P],
                                               x1[:, BPH * h + b, (4 * j + k) * P:(4 * j + k + 1) * P],
                                               ident[:, :])
                        mm.then_inc(t_mm, 1)
                eng.wait_ge(t_ev, 2 * BPH * (h + 1))

                def scores(jj, i):
                    n = jj * 8 + (QT * h + i)
                    eng.wait_ge(q_ev, n + 3)
                    eng.wait_ge(sc_ev, n + 1)
                    for b in range(BPH):
                        mm = eng.matmul(ps[:, 4 + i % 2, b * P:(b + 1) * P], q_s[:, i % 2, b * P:(b + 1) * P],
                                        keys[:, bass.ds(jj * 8 + i, 1), :].rearrange("p a n -> p (a n)"),
                                        start=True, stop=True)
                    mm.then_inc(sc_mm, 1)

                with eng.Fori(0, QT // 8) as jj:
                    for i in range(8):
                        if i % 4 == 0:
                            eng.wait_ge(w_in[i // 4], jj * 16 + 16 * (8 * h + 7))
                        eng.wait_ge(q_ev, jj * 8 + (QT * h + i + 1))
                        project(2 + i % 2, wtile(w_buf[i // 4], i % 4), x1t, q_mm)
                        if i:
                            scores(jj, i - 1)
                    scores(jj, 7)

            def seed(b):
                eng.wait_ge(out_ev, b + 1)
                for j in range(2):
                    eng.matmul(ps[:, j, :], ident_a[:, :],
                               x1[:, bass.ds(b, 1), j * HALF:(j + 1) * HALF].rearrange("p a d -> p (a d)"),
                               start=True, stop=True)

            def head(g):
                for c in range(2):
                    for s in range(RING):
                        eng.wait_ge(diag_ready, g * (2 * RING) + (c * RING + s + 1))
                        eng.wait_ge(v_in[s], g * 32 + 16 * (c + 1))
                        for j in range(2):
                            mm = eng.matmul(ps[:, j, :], diag[:, s, :], v_ring[s][:, j * HALF:(j + 1) * HALF],
                                            start=False, stop=False, skip_group_check=True)
                        mm.then_inc(v_used, 1)

            with eng.Fori(0, NBLK) as b:
                seed(b)
                with eng.Fori(0, HEADS) as hd:
                    head(b * HEADS + hd)

        @block.vector
        def _(eng):
            eng.sem_inc(mix_ev, 1)
            eng.sem_inc(y_done, 1)
            eng.sem_inc(sc_ev, 2)
            eng.sem_inc(u_used, RING)
            eng.memset(halo[:, :, :], 0.0)
            eng.memset(h_last[:, :], 0.0)

            lam = chan[:, LAM, :]
            eng.wait_ge(const_in, 64)
            eng.tensor_scalar(sp[:, 5, :], lam, -1.0, None, ALU.mult)
            eng.drain()
            eng.tensor_tensor(sp[:, 0, :], lam, sp[:, 5, :], ALU.max).then_inc(lam_abs, 1)
            eng.wait_ge(lam_exp, 1)
            eng.tensor_scalar(sp[:, 2, :], sp[:, 1, :], 2.0, None, ALU.add)
            eng.drain()
            eng.reciprocal(sp[:, 2, :], sp[:, 2, :])
            eng.drain()
            eng.tensor_tensor(sp[:, 2, :], sp[:, 1, :], sp[:, 2, :], ALU.mult)
            eng.drain()
            eng.tensor_tensor(sp[:, 3, :], sp[:, 2, :], sp[:, 2, :], ALU.mult)
            terms = 9
            eng.drain()
            eng.tensor_scalar(sp[:, 4, :], sp[:, 3, :], 2.0 / (2 * terms + 1), 2.0 / (2 * terms - 1),
                              ALU.mult, ALU.add)
            for k in range(terms - 2, -1, -1):
                eng.drain()
                eng.tensor_tensor(sp[:, 4, :], sp[:, 4, :], sp[:, 3, :], ALU.mult)
                eng.drain()
                eng.tensor_scalar(sp[:, 4, :], sp[:, 4, :], 2.0 / (2 * k + 1), None, ALU.add)
            eng.drain()
            eng.tensor_tensor(sp[:, 4, :], sp[:, 4, :], sp[:, 2, :], ALU.mult)
            eng.tensor_scalar(sp[:, 5, :], sp[:, 5, :], 0.0, None, ALU.max)
            eng.drain()
            eng.tensor_tensor(sp[:, 4, :], sp[:, 4, :], sp[:, 5, :], ALU.add)
            eng.drain()
            eng.tensor_scalar(dec[:, 0, :], sp[:, 4, :], -LRU_C, None, ALU.mult)
            eng.tensor_scalar(dec[:, 1, :], sp[:, 4, :], LRU_C, None, ALU.mult).then_inc(dec_ready, 1)
            eng.wait_ge(masks, 1)
            eng.tensor_scalar(ident_a[:, :], ident[:, :], ALPHA, None, ALU.mult)

            def variance(lo, hi):
                eng.drain()
                for b in range(lo, hi):
                    eng.bn_aggr(mv[:, b, :], stats[:, b, :, :])
                eng.drain()
                eng.tensor_scalar(rstd[:, lo:hi], mv[:, lo:hi, 1], EPS, None, ALU.add).then_inc(var_ready, 1)

            def inverse(lo, hi, n):
                eng.drain()
                eng.wait_ge(std_ready, n)
                eng.reciprocal(rstd[:, lo:hi], rstd[:, lo:hi])
                eng.drain()

            def normalise(data, b):
                eng.tensor_scalar(data, data, mv[:, b, 0:1], rstd[:, b:b + 1], ALU.subtract, ALU.mult)
                eng.drain()
                eng.tensor_tensor(data, data, ln_gb[:, 0, :], ALU.mult)
                eng.drain()
                return eng.tensor_tensor(data, data, ln_gb[:, 1, :], ALU.add)

            def convolve(h, c):
                n = c + (CT * h + 1)
                ch = lambda row: chan[:, row, bass.ds(c, 1)]
                hal = halo[:, bass.ds(c, 1), :].rearrange("p a k -> p (a k)")
                eng.drain()
                eng.tensor_copy(xa[:, 0:CONV - 1], hal)
                eng.drain()
                eng.wait_ge(xa_ev, n + 1)
                eng.tensor_scalar(xc[:, :], xa[:, CONV - 1:], ch(CW + CONV - 1), ch(CB), ALU.mult, ALU.add)
                for k in range(CONV - 1):
                    eng.drain()
                    step = eng.scalar_tensor_tensor(out=xc[:, :], in0=xa[:, k:k + HALF], scalar=ch(CW + k),
                                                    in1=xc[:, :], op0=ALU.mult, op1=ALU.add)
                step.then_inc(xc_ready, 1)
                eng.tensor_copy(hal, xa[:, HALF:HALF + CONV - 1])

            def recur_and_merge(h, c):
                n = c + (CT * h + 1)
                eng.drain()
                eng.wait_ge(decay, n)
                eng.scalar_tensor_tensor(out=rr[:, :], in0=a2[:, :], scalar=1.0, in1=rr[:, :],
                                         op0=ALU.add, op1=ALU.mult).then_inc(one_less, 1)
                eng.tensor_tensor(ii[:, :], ii[:, :], xc[:, :], ALU.mult)
                eng.drain()
                eng.wait_ge(root, n)
                eng.tensor_tensor(ii[:, :], ii[:, :], rr[:, :], ALU.mult)
                eng.drain()
                eng.tensor_tensor_scan(a2[:, :], aa[:, :], ii[:, :], h_last[:, bass.ds(c, 1)],
                                       ALU.mult, ALU.add)
                eng.drain()
                eng.tensor_copy(h_last[:, bass.ds(c, 1)], a2[:, HALF - 1:HALF])
                eng.tensor_tensor(gg[:, :], gg[:, :], a2[:, :], ALU.mult)
                eng.drain()
                eng.wait_ge(g_a_ev, n + 1)
                eng.tensor_tensor(gg[:, :], gg[:, :], s_a[:, :], ALU.mult)
                eng.wait_ge(mix_mm, n + 1)
                bias = bs_b[:, bass.ds(c, 1), :].to_broadcast([P, BPH, P])
                eng.tensor_tensor(xc[:, :].rearrange("p (b t) -> p b t", b=BPH),
                                  ps[:, MIX, :].rearrange("p (b t) -> p b t", b=BPH), bias,
                                  ALU.add).then_inc(mix_ev, 1)
                eng.drain()
                eng.tensor_tensor(xc[:, :], xc[:, :], gu[:, :], ALU.mult)
                eng.drain()
                eng.wait_ge(g_b_ev, n + 1)
                eng.tensor_tensor(xc[:, :], xc[:, :], s_b[:, :], ALU.mult)
                eng.drain()
                eng.tensor_tensor(y_t[:, bass.ds(c, 1), :].rearrange("p a t -> p (a t)"),
                                  gg[:, :], xc[:, :], ALU.add).then_inc(y_done, 1)

            def top_keys(h, jj, i):
                n = jj * 8 + (QT * h + i)
                score = lambda b: ps[:, 4 + i % 2, b * P:(b + 1) * P]
                wait_alone(eng, sc_mm, n + 1)
                eng.drain()
                for b in range(BPH):
                    eng.max(top_st[:, b, i, 0:8], score(b))
                eng.drain()
                for b in range(BPH):
                    eng.match_replace(knock[:, b, :], top_st[:, b, i, 0:8], score(b), LOWEST)
                for b in range(BPH):
                    eng.max_index(key_st[:, b, i, 0:8], top_st[:, b, i, 0:8], score(b))
                eng.drain()
                for b in range(BPH):
                    eng.max(top_st[:, b, i, 8:16], knock[:, b, :])
                eng.drain()
                for b in range(BPH):
                    last = eng.max_index(key_st[:, b, i, 8:16], top_st[:, b, i, 8:16], knock[:, b, :])
                last.then_inc(sc_ev, 1)

            for h in range(NHALF):
                for n in range(2 * BPH):
                    half, b = divmod(n, BPH)
                    eng.wait_ge(v_gelu, 2 * BPH * h + n + 1)
                    eng.bn_stats(stats[:, b, half, :], v_tok[:, b, half * HALF:(half + 1) * HALF])
                eng.wait_ge(ln_in, 32 * (2 * h + 1))
                variance(0, BPH)
                convolve(h, 0)
                inverse(0, BPH, (BPH + 1) * h + 1)
                for b in range(BPH):
                    step = normalise(v_tok[:, b, :], b)
                step.then_inc(v_norm, 1)
                recur_and_merge(h, 0)
                with eng.Fori(1, CT) as c:
                    convolve(h, c)
                    recur_and_merge(h, c)
                eng.wait_ge(x_in, 16 * (h + 1))
                eng.wait_ge(ln_in, 32 * (2 * h + 2))
                for n in range(2 * BPH):
                    half, b = divmod(n, BPH)
                    part = x1[:, BPH * h + b, half * HALF:(half + 1) * HALF]
                    eng.wait_ge(o_mm, 2 * BPH * h + n + 1)
                    eng.scalar_tensor_tensor(out=part, in0=part, scalar=ALPHA, in1=ps[:, 4 + n % 2, :],
                                             op0=ALU.mult, op1=ALU.add).then_inc(o_ev, 1)
                    eng.drain()
                    eng.bn_stats(stats[:, b, half, :], part)
                    if half:
                        variance(b, b + 1)
                        inverse(b, b + 1, (BPH + 1) * h + 2 + b)
                        normalise(x1[:, BPH * h + b, :], b).then_inc(x1_ready, 1)
                with eng.Fori(0, QT // 8) as jj:
                    for i in range(8):
                        top_keys(h, jj, i)
                    eng.drain()
                    for dst, src in ((top_v, top_st), (top_i, key_st)):
                        for b in range(BPH):
                            eng.tensor_copy(dst[:, bass.ds(jj * 4 + (BPH * h + b) * HEADS, 4), :, :].rearrange(
                                "p g a k -> p (g a k)"), src[:, b, :, :].rearrange("p i k -> p (i k)"))
                    eng.drain()

            def select(g):
                val = top_v[:, bass.ds(g, 1), :, :].rearrange("p g a k -> p (g a) k")
                key = top_i[:, bass.ds(g, 1), :, :].rearrange("p g a k -> p (g a) k")
                grid = [P, TOPK, TOPK]
                eng.drain()
                eng.tensor_tensor(cand[:, :].rearrange("p (a b) -> p a b", a=TOPK),
                                  val[:, 0, :].unsqueeze(2).to_broadcast(grid),
                                  val[:, 1, :].unsqueeze(1).to_broadcast(grid), ALU.add)
                eng.drain()
                eng.max(best[:, 0:8], cand[:, :])
                eng.drain()
                eng.match_replace(cand2[:, :], best[:, 0:8], cand[:, :], LOWEST)
                eng.max_index(pos[:, 0:8], best[:, 0:8], cand[:, :])
                eng.drain()
                eng.max(best[:, 8:16], cand2[:, :])
                eng.drain()
                eng.max_index(pos[:, 8:16], best[:, 8:16], cand2[:, :])
                eng.tensor_scalar(less[:, :], best[:, :], best[:, 0:1], None, ALU.subtract
                                  ).then_inc(less_ready, 1)
                eng.drain()
                eng.tensor_scalar(pair[:, 0, :], pos[:, :], 4, None, ALU.logical_shift_right)
                eng.tensor_scalar(pair[:, 1, :], pos[:, :], TOPK - 1, None, ALU.bitwise_and)
                eng.drain()
                quad = [P, 2, TOPK, TOPK]
                eng.tensor_tensor(hot[:, :, :, :], pair[:, :, :].unsqueeze(3).to_broadcast(quad),
                                  iota[:, :].unsqueeze(1).unsqueeze(1).to_broadcast(quad), ALU.is_equal)
                eng.drain()
                eng.tensor_tensor(hot[:, :, :, :], hot[:, :, :, :],
                                  key.unsqueeze(2).to_broadcast(quad), ALU.mult)
                eng.drain()
                eng.tensor_reduce(picked[:, :, :], hot[:, :, :, :], AX_X, ALU.add)
                eng.drain()
                eng.scalar_tensor_tensor(out=ids[:, bass.ds(g, 1), :].rearrange("p g k -> p (g k)"),
                                         in0=picked[:, 0, :], scalar=float(NKEY), in1=picked[:, 1, :],
                                         op0=ALU.mult, op1=ALU.add).then_inc(ids_ready, 1)

            def gate(g):
                eng.drain()
                eng.wait_ge(exp_done, g + 1)
                eng.tensor_reduce(tot[:, 0:1], expo[:, :], AX_X, ALU.add)
                eng.drain()
                eng.reciprocal(tot[:, 1:2], tot[:, 0:1])
                eng.drain()
                eng.tensor_scalar(gates[:, bass.ds(g * TOPK, TOPK)], expo[:, :], tot[:, 1:2], None, ALU.mult)
                eng.drain()

            def dots(g, c):
                for s in range(RING):
                    eng.wait_ge(u_in[s], g * 32 + 16 * (c + 1))
                    eng.tensor_tensor_reduce(u_ring[s], u_ring[s], x1_now, 1.0, 0.0, ALU.mult, ALU.add,
                                             hdot[:, c, s:s + 1]).then_inc(u_used, 1)

            def diagonals(g, c):
                wait_alone(eng, gelu_done, g * 2 + (c + 1))
                eng.drain()
                eng.tensor_tensor(wact[:, :], hact[:, c, :], gates[:, bass.ds(g * TOPK + c * RING, RING)],
                                  ALU.mult)
                eng.drain()
                for s in range(RING):
                    eng.wait_ge(v_used, g * (2 * RING) + (c * RING + s + 1))
                    eng.tensor_scalar(diag[:, s, :], ident[:, :], wact[:, s:s + 1], None, ALU.mult
                                      ).then_inc(diag_ready, 1)

            def take_block(b):
                eng.drain()
                eng.tensor_copy(x1_now, x1[:, bass.ds(b, 1), :].rearrange("p a d -> p (a d)"))
                eng.drain()

            def finish(b):
                wait_alone(eng, out_ev, b + 2)
                eng.drain()
                for j in range(2):
                    eng.bn_stats(stats[:, 0, j, :], res[:, j * HALF:(j + 1) * HALF])
                variance(0, 1)
                inverse(0, 1, b + ((BPH + 1) * NHALF + 1))
                normalise(res, 0).then_inc(fin, 1)

            def head(g, chosen=True, first=False, done=None):
                dots(g, 0)
                if not first:
                    diagonals(g - 1, 1)
                if chosen:
                    select(g + LEAD)
                dots(g, 1)
                diagonals(g, 0)
                if done is not None:
                    finish(done)
                if chosen:
                    gate(g + LEAD)

            eng.wait_ge(ln_in, 32 * (2 * NHALF + 1))
            with eng.Fori(0, LEAD) as g:
                select(g)
                gate(g)
            take_block(0)
            head(0, first=True)
            with eng.Fori(1, HEADS) as g:
                head(g)
            with eng.Fori(1, NBLK - 1) as b:
                take_block(b)
                head(b * HEADS, done=b - 1)
                with eng.Fori(1, HEADS) as hd:
                    head(b * HEADS + hd)
            last = HEADS * (NBLK - 1)
            take_block(NBLK - 1)
            head(last, done=NBLK - 2)
            with eng.Fori(last + 1, NG - LEAD) as g:
                head(g)
            with eng.Fori(NG - LEAD, NG) as g:
                head(g, chosen=False)
            diagonals(NG - 1, 1)
            finish(NBLK - 1)


def kernel(**inputs):
    import numpy as np
    import concourse.bacc as bacc
    from concourse.bass_utils import run_bass_kernel_spmd

    a = {k: np.asarray(v) for k, v in inputs.items()}

    def tiles(w):
        return w.reshape(KT, P, -1, P).transpose(2, 1, 0, 3)

    def halves(w):
        return w.reshape(KT, P, 2, HALF).transpose(2, 1, 0, 3).reshape(2, P, KT * HALF)

    w_in = a["w_in"][0]
    wt = tiles(w_in)
    parts = [wt[CT * j:CT * (j + 1)].reshape(CT, P, TILE) for j in (0, 1, 2, 4, 5)]
    parts += [a["rg_w_a"][0], a["rg_w_x"][0]]
    cols = np.concatenate([a["conv_w"][0], a["conv_b"], a["rg_b_a"], a["rg_b_x"], a["rg_lambda"],
                           a["b_gate"][0]])
    arrays = {
        "x": a["x"][0],
        "x_t": a["x"][0].T.reshape(KT, P, NHALF, HALF).transpose(2, 1, 0, 3).reshape(NHALF, P, KT * HALF),
        "w_mix": np.concatenate(parts, axis=2),
        "w_v": halves(w_in[:, 3 * D:4 * D]),
        "w_out": halves(a["w_out"][0]),
        "w_q": tiles(a["peer_wq"][0]).reshape(4, 4, P, TILE).transpose(0, 2, 1, 3).reshape(4, P, 4 * TILE),
        "keys_t": a["peer_sub_keys"][0].reshape(QT, NKEY, P).transpose(2, 0, 1),
        "ws_t": a["gm_ws"][0].transpose(2, 0, 1),
        "bs": a["gm_bs"][0].reshape(-1),
        "chan": cols.reshape(NCHAN, CT, P).transpose(2, 0, 1),
        "ln": np.stack([np.stack([a[g][0], a[b][0]]) for g, b in
                        (("gm_ln_g", "gm_ln_b"), ("ln1_g", "ln1_b"), ("ln2_g", "ln2_b"))]),
        "peer_u": a["peer_u"][0],
        "peer_v": a["peer_v"][0],
    }
    arrays = {f"{k}_dram": np.ascontiguousarray(v) for k, v in arrays.items()}
    nc = bacc.Bacc("TRN2", target_bir_lowering=False, num_devices=1)
    args = [nc.dram_tensor(k, v.shape, mybir.dt.from_np(v.dtype), kind="ExternalInput").ap()
            for k, v in arrays.items()]
    out = nc.dram_tensor("out_dram", (T, D), F32, kind="ExternalOutput").ap()
    build(nc, *args, out)
    r = run_bass_kernel_spmd(nc, [arrays], core_ids=[0])
    return r.results[0]["out_dram"].reshape(1, T, D)
```

```python
from contextlib import ExitStack

import concourse.bass as bass
from concourse import mybir

ALU = mybir.AluOpType
ACT = mybir.ActivationFunctionType
F32 = mybir.dt.float32
U32 = mybir.dt.uint32
U16 = mybir.dt.uint16
AX_X = mybir.AxisListType.X

P = 128
D = 1024
T = 1024
KT = D // P
CT = D // P
HALF = 512
NHALF = T // HALF
BPH = HALF // P
NBLK = T // P
HEADS = 8
NKEY = 128
TOPK = 16
QT = 2 * HEADS
NG = NBLK * HEADS
RING = 8
LEAD = 3
CONV = 4
LRU_C = 8.0
ALPHA = 2.0 ** 0.25
EPS = 1e-5
LOWEST = -3.0e38
TILE = KT * P
QW = TILE + P
GBW = TILE + 2 * P
CW, CB, BA, BX, LAM, BGA, BGB = 0, 4, 5, 6, 7, 8, 9
NCHAN = 10
XA, GA, R, I, U, G_A, MIX, G_B = 2, 3, 2, 3, 4, 5, 6, 7
V_BANK, O_BANK, Q_BANK, SC_BANK = 6, 4, 2, 4
Q_STEPS = ((0, 1), (2, 3), (4,), (5,), (6,), (7,), (), ())
SC_STEPS = ((),) + Q_STEPS[:-1]


def build(nc, x, x_t, w_mix, w_gb, w_v, w_out, w_q, ws_t, bs, chan_d, ln_d, peer_u, peer_v, x1_d, out):
    with ExitStack() as ctx:
        def sb(name, shape, dt=F32):
            return ctx.enter_context(nc.sbuf_tensor(name, shape, dt))

        def sem(name):
            return ctx.enter_context(nc.semaphore(name))

        w_area = sb("w_area", [P, 4 * QW + GBW])
        w_slot = [w_area[:, j * QW:(j + 1) * QW] for j in range(4)] + [w_area[:, 4 * QW:]]
        x_area = sb("x_area", [P, KT * HALF])
        xt = x_area[:, :].rearrange("p (k t) -> p k t", k=KT)
        x1 = x_area[:, :].rearrange("p (b d) -> p b d", b=BPH)
        v_area = sb("v_area", [P, KT * HALF])
        v_tok = v_area[:, :].rearrange("p (b c) -> p b c", b=BPH)
        x1t = v_area[:, :].rearrange("p (k t) -> p k t", k=KT)
        u_area, v_rows = sb("u_area", [P, RING, D]), sb("v_rows", [P, RING, D])
        u_ring = [u_area[:, s, :] for s in range(RING)]
        v_ring = [v_rows[:, s, :] for s in range(RING)]
        diag = sb("diag", [P, RING, P])
        x1_next, x1_now = sb("x1_next", [P, D]), sb("x1_now", [P, D])
        res = sb("res", [P, D])

        ws = sb("ws", [P, CT, P])
        bs_b = sb("bs_b", [P, CT, P])
        ln_gb = sb("ln_gb", [P, 2, D])
        ln2_gb = sb("ln2_gb", [P, 2, D])
        chan = sb("chan", [P, NCHAN, CT])
        xa = sb("xa", [P, CONV - 1 + HALF])
        halo = sb("halo", [P, CT, CONV - 1])
        h_last = sb("h_last", [P, CT])
        xc, gg, rr, ii, aa, a2, gu, s_a, s_b = (
            sb(n, [P, HALF]) for n in ("xc", "gg", "rr", "ii", "aa", "a2", "gu", "s_a", "s_b"))
        v_st = sb("v_st", [P, BPH, P])
        q_s = [gg, rr]
        knock = ii[:, :].rearrange("p (b n) -> p b n", b=BPH)
        top_st = s_a[:, :].rearrange("p (b i k) -> p b i k", b=BPH, i=8)
        key_st = s_b[:, :].bitcast(U16)[:, 0:HALF].rearrange("p (b i k) -> p b i k", b=BPH, i=8)
        top_v = sb("top_v", [P, NG, 2, TOPK])
        top_i = sb("top_i", [P, NG, 2, TOPK], U16)
        ids = sb("ids", [P, NG, TOPK], U16)
        gates = sb("gates", [P, NG * TOPK])
        id_now = sb("id_now", [P, 2, TOPK], U32)
        cand = sb("cand", [P, TOPK * TOPK])
        cand2 = sb("cand2", [P, TOPK * TOPK])
        best = sb("best", [P, TOPK])
        pos = sb("pos", [P, TOPK], U32)
        pair = sb("pair", [P, 2, TOPK], U32)
        hot = sb("hot", [P, 2, TOPK, TOPK])
        picked = sb("picked", [P, 2, TOPK])
        less = sb("less", [P, TOPK])
        expo = sb("expo", [P, TOPK])
        tot = sb("tot", [P, 2])
        hdot = sb("hdot", [P, 2, RING])
        hact = sb("hact", [P, 2, RING])
        wact = sb("wact", [P, RING])
        ident = sb("ident", [P, P])
        ident_a = sb("ident_a", [P, P])
        iota = sb("iota", [P, TOPK], U32)
        stats = sb("stats", [P, BPH, 2, 6])
        mv = sb("mv", [P, BPH, 2])
        rstd = sb("rstd", [P, BPH])
        stats2, mv2, rstd2 = sb("stats2", [P, 2, 6]), sb("mv2", [P, 2]), sb("rstd2", [P, 1])
        sp = sb("sp", [P, 6, CT])
        dec = sb("dec", [P, 2, CT])
        ps = ctx.enter_context(nc.psum_tensor("ps", [P, 8, HALF], F32))

        const_in, xt_in, x_in, ln_in = sem("const_in"), sem("xt_in"), sem("x_in"), sem("ln_in")
        w_in = [sem(f"w_in{j}") for j in range(5)]
        masks = sem("masks")
        lam_abs, lam_exp, dec_ready = sem("lam_abs"), sem("lam_exp"), sem("dec_ready")
        v_mm, v_gelu, v_norm = sem("v_mm"), sem("v_gelu"), sem("v_norm")
        xa_mm, ga_mm, ri_mm, u_mm, mix_mm, g_a_mm, g_b_mm = (
            sem(n) for n in ("xa_mm", "ga_mm", "ri_mm", "u_mm", "mix_mm", "g_a_mm", "g_b_mm"))
        xa_ev, ga_ev, ri_ev, u_ev, mix_ev, g_a_ev, g_b_ev = (
            sem(n) for n in ("xa_ev", "ga_ev", "ri_ev", "u_ev", "mix_ev", "g_a_ev", "g_b_ev"))
        kept = sem("kept")
        x1_stored = sem("x1_stored")
        xc_ready, decay = sem("xc_ready"), sem("decay")
        one_less, root = sem("one_less"), sem("root")
        var_ready, std_ready = sem("var_ready"), sem("std_ready")
        y_done = sem("y_done")
        st_ready = sem("st_ready")
        o_mm, o_ev, x1_ready, t_mm, t_ev = (
            sem(n) for n in ("o_mm", "o_ev", "x1_ready", "t_mm", "t_ev"))
        q_mm, sc_mm = sem("q_mm"), sem("sc_mm")
        q_ev, sc_ev = sem("q_ev"), sem("sc_ev")
        ids_ready, less_ready, exp_done = sem("ids_ready"), sem("less_ready"), sem("exp_done")
        id_copied = sem("id_copied")
        u_in = [sem(f"u_in{s}") for s in range(RING)]
        v_in = [sem(f"v_in{s}") for s in range(RING)]
        u_used, v_used = sem("u_used"), sem("v_used")
        gelu_done, diag_ready = sem("gelu_done"), sem("diag_ready")
        out_ev = sem("out_ev")
        next_in, taken = sem("next_in"), sem("taken")
        fin_var, fin_std, fin = sem("fin_var"), sem("fin_std"), sem("fin")
        stored = sem("stored")
        tick = sem("tick")

        def wait_alone(eng, s, value):
            eng.wait_ge(s, value)
            eng.sem_inc(tick, 1)

        def wtile(j):
            return w_slot[j][:, 0:TILE].rearrange("p (k c) -> p k c", k=KT)

        def wrow(k):
            return w_slot[k // 2][:, (k % 2) * HALF:(k % 2 + 1) * HALF]

        block = ctx.enter_context(nc.Block())

        @block.sync
        def _(eng):
            def load_ln(dst, n, landed):
                for j in range(2):
                    eng.dma_start(dst[:, j, :], ln_d[n, j].partition_broadcast(P)).then_inc(landed, 16)

            def load_half(w, half):
                for j in range(4):
                    eng.dma_start(w_slot[j][:, 0:TILE], w[half][:, j * TILE:(j + 1) * TILE]
                                  ).then_inc(w_in[j], 16)

            def load_mix(c, j):
                src = w_mix[j] if j < 4 else w_gb
                eng.dma_start(w_slot[j][:, 0:TILE if j < 4 else GBW],
                              src[bass.ds(c, 1)].rearrange("a p n -> (a p) n")).then_inc(w_in[j], 16)

            for h in range(NHALF):
                if h:
                    eng.wait_ge(t_mm, 2 * BPH * h)
                    eng.wait_ge(x1_stored, 16 * h)
                eng.dma_start(xt, x_t[h].rearrange("p (k t) -> p k t", k=KT)).then_inc(xt_in, 16)
                if h:
                    eng.wait_ge(q_mm, QT * h)
                    eng.wait_ge(sc_mm, QT * h)
                load_half(w_v, 0)
                if h == 0:
                    eng.dma_start(chan[:, :, :], chan_d).then_inc(const_in, 16)
                    eng.dma_start(ws[:, :, :], ws_t).then_inc(const_in, 16)
                    eng.dma_start(bs_b[:, :, :].rearrange("p c t -> p (c t)"),
                                  bs.partition_broadcast(P)).then_inc(const_in, 16)
                    load_ln(ln_gb, 0, ln_in)
                    load_ln(ln2_gb, 2, const_in)
                eng.wait_ge(v_mm, 2 * BPH * h + BPH)
                load_half(w_v, 1)
                if h:
                    eng.wait_ge(g_b_mm, CT * h)
                load_mix(0, 4)
                eng.wait_ge(v_mm, 2 * BPH * (h + 1))
                for j in range(4):
                    load_mix(0, j)
                with eng.Fori(1, CT) as c:
                    for j, used in enumerate((xa_mm, ga_mm, u_mm, g_a_mm, g_b_mm)):
                        eng.wait_ge(used, c + CT * h)
                        load_mix(c, j)
                eng.wait_ge(v_norm, h + 1)
                load_ln(ln_gb, 1, ln_in)
                eng.wait_ge(g_a_mm, CT * (h + 1))
                load_half(w_out, 0)
                eng.wait_ge(g_b_mm, CT * (h + 1))
                eng.dma_start(x1, x[h * HALF:(h + 1) * HALF, :].rearrange("(b p) d -> p b d", p=P)
                              ).then_inc(x_in, 16)
                eng.wait_ge(o_mm, 2 * BPH * h + BPH)
                load_half(w_out, 1)
                eng.wait_ge(o_mm, 2 * BPH * (h + 1))
                for j in range(4):
                    eng.dma_start(w_slot[j], w_q[j]).then_inc(w_in[j], 16)
                eng.wait_ge(x1_ready, BPH * (h + 1))
                eng.dma_start(x1_d[h * HALF:(h + 1) * HALF, :].rearrange("(b p) d -> p b d", p=P),
                              x1).then_inc(x1_stored, 16)
                if h < NHALF - 1:
                    load_ln(ln_gb, 0, ln_in)
                with eng.Fori(1, QT // 4) as i4:
                    for j in range(4):
                        eng.wait_ge(sc_mm, i4 * 4 + (QT * h + j - 3))
                        eng.dma_start(w_slot[j], w_q[bass.ds(i4 * 4 + j, 1)].rearrange(
                            "a p n -> (a p) n")).then_inc(w_in[j], 16)

        @block.gpsimd
        def _(eng):
            eng.memset(ident[:, :], 0.0)
            eng.iota(iota[:, :], pattern=[[1, TOPK]], base=0, channel_multiplier=0)
            eng.drain()
            eng.affine_select(out=ident[:, :], in_=ident[:, :], compare_op=ALU.not_equal, fill=1.0,
                              base=0, pattern=[[-1, P]], channel_multiplier=1)
            eng.wait_ge(const_in, 16 * 5)
            eng.affine_select(out=ws[:, :, :], in_=ws[:, :, :], compare_op=ALU.is_ge, fill=0.0,
                              base=0, pattern=[[0, CT], [1, P]], channel_multiplier=-1
                              ).then_inc(masks, 1)

            def gather(ring, landed, table, used, par, g, c, s):
                wait_alone(eng, used, g * (2 * RING) + (c * RING + s + 1))
                eng.indirect_dma_start(ring[s], None, table, bass.IndirectOffsetOnAxis(
                    ap=id_now[:, par, c * RING + s:c * RING + s + 1], axis=0)).then_inc(landed[s], 16)

            def gather_u(par, g, c):
                for s in range(RING):
                    gather(u_ring, u_in, peer_u, u_used, par, g, c, s)

            def gather_v(par, g, c):
                for s in range(RING):
                    gather(v_ring, v_in, peer_v, v_used, par, g, c, s)

            def head(par, g, first=False):
                wait_alone(eng, ids_ready, g + 1)
                eng.tensor_copy(id_now[:, par, :], ids[:, bass.ds(g, 1), :].rearrange(
                    "p a k -> p (a k)")).then_inc(id_copied, 1)
                eng.drain()
                gather_u(par, g, 0)
                if not first:
                    gather_v(1 - par, g - 1, 1)
                gather_u(par, g, 1)
                gather_v(par, g, 0)

            head(0, 0, first=True)
            head(1, 1)
            with eng.Fori(1, NG // 2) as gg2:
                head(0, gg2 * 2)
                head(1, gg2 * 2 + 1)
            gather_v(1, NG - 1, 1)
            for s in range(RING):
                eng.wait_ge(v_in[s], 16 * 2 * NG)

        @block.scalar
        def _(eng):
            for s in (xa_ev, ga_ev, ri_ev, u_ev, g_a_ev, g_b_ev, out_ev):
                eng.sem_inc(s, 1)
            eng.sem_inc(q_ev, 2)
            eng.wait_ge(lam_abs, 1)
            eng.activation(sp[:, 1, :], sp[:, 0, :], ACT.Exp, scale=-1.0).then_inc(lam_exp, 1)

            def std(lo, hi, n):
                wait_alone(eng, var_ready, n)
                eng.activation(rstd[:, lo:hi], rstd[:, lo:hi], ACT.Sqrt).then_inc(std_ready, 1)

            def a1(h, step):
                for n in ((), (0, 1), (2,), (3,), (4,), (5,), (6,), (7,))[step]:
                    eng.wait_ge(v_mm, 2 * BPH * h + n + 1)
                    eng.activation(v_tok[:, n % BPH, (n // BPH) * HALF:(n // BPH + 1) * HALF],
                                   ps[:, V_BANK + n % 2, :], ACT.Gelu_apprx_tanh).then_inc(v_gelu, 1)
                if step == 7:
                    std(0, BPH, (BPH + 1) * h + 1)

            def a2_step(h, c, step):
                n = c + (CT * h + 1)
                ch = lambda row: chan[:, row, bass.ds(c, 1)]
                if step == 1:
                    wait_alone(eng, y_done, n)
                    wait_alone(eng, xa_mm, n)
                    eng.activation(xa[:, CONV - 1:], ps[:, XA, :], ACT.Copy).then_inc(xa_ev, 1)
                    wait_alone(eng, ga_mm, n)
                    eng.activation(gg[:, :], ps[:, GA, :], ACT.Gelu_apprx_tanh).then_inc(ga_ev, 1)
                    wait_alone(eng, mix_mm, n)
                    eng.wait_ge(v_norm, h + 1)
                    eng.activation(v_st[:, :, :], v_tok[:, :, bass.ds(c * P, P)], ACT.Copy
                                   ).then_inc(st_ready, 1)
                if step == 2:
                    wait_alone(eng, u_mm, n)
                    eng.activation(gu[:, :], ps[:, U, :], ACT.Gelu_apprx_tanh).then_inc(u_ev, 1)
                    wait_alone(eng, g_a_mm, n)
                    eng.activation(s_a[:, :], ps[:, G_A, :], ACT.Sigmoid, bias=ch(BGA)).then_inc(g_a_ev, 1)
                if step == 3:
                    wait_alone(eng, ri_mm, n)
                    eng.activation(rr[:, :], ps[:, R, :], ACT.Sigmoid, bias=ch(BA))
                    eng.activation(ii[:, :], ps[:, I, :], ACT.Sigmoid, bias=ch(BX)).then_inc(ri_ev, 1)
                    eng.drain()
                    eng.activation(aa[:, :], rr[:, :], ACT.Exp, scale=dec[:, 0, bass.ds(c, 1)])
                    eng.drain()
                    eng.activation(rr[:, :], rr[:, :], ACT.Tanh, scale=dec[:, 1, bass.ds(c, 1)])
                    eng.activation(a2[:, :], aa[:, :], ACT.Square).then_inc(decay, 1)
                    wait_alone(eng, one_less, n)
                    eng.activation(rr[:, :], rr[:, :], ACT.Sqrt).then_inc(root, 1)
                    wait_alone(eng, g_b_mm, n)
                    eng.activation(s_b[:, :], ps[:, G_B, :], ACT.Sigmoid, bias=ch(BGB)).then_inc(g_b_ev, 1)

            def a3(h, step):
                if step in (3, 4):
                    for b in (2 * step - 6, 2 * step - 5):
                        std(b, b + 1, (BPH + 1) * h + 2 + b)
                if step in (5, 6):
                    for b in (2 * step - 10, 2 * step - 9):
                        for j in range(2):
                            eng.wait_ge(t_mm, 2 * (BPH * h + b) + j + 1)
                            eng.activation(x1t[:, 4 * j:4 * j + 4, b * P:(b + 1) * P],
                                           ps[:, 2 + 4 * (b % 2) + j, :].rearrange("p (k t) -> p k t", k=4),
                                           ACT.Copy).then_inc(t_ev, 1)

            def a4(h, jj, step):
                for i in SC_STEPS[step]:
                    n = jj * 8 + (QT * h + i)
                    wait_alone(eng, q_mm, n + 1)
                    wait_alone(eng, sc_ev, n + 1)
                    eng.activation(q_s[i % 2][:, :], ps[:, Q_BANK + i % 2, :], ACT.Copy).then_inc(q_ev, 1)

            def softmax_exp(g):
                wait_alone(eng, less_ready, g + 1)
                eng.activation(expo[:, :], less[:, :], ACT.Exp).then_inc(exp_done, 1)

            def gelu(g, c):
                wait_alone(eng, u_used, g * (2 * RING) + (RING * (c + 1) + RING))
                eng.activation(hact[:, c, :], hdot[:, c, :], ACT.Gelu_apprx_tanh).then_inc(gelu_done, 1)

            def load_next(b):
                eng.dma_start(x1_next[:, :], x1_d[bass.ds(b * P, P), :]).then_inc(next_in, 16)

            def store(b):
                wait_alone(eng, fin, b + 1)
                eng.dma_start(out[bass.ds(b * P, P), :], res[:, :]).then_inc(stored, 16)
                wait_alone(eng, stored, b * 16 + 16)

            def evacuate(b):
                wait_alone(eng, v_used, b * (HEADS * TOPK) + (HEADS * TOPK + RING))
                eng.activation(res[:, 0:HALF], ps[:, 0, :], ACT.Copy)
                eng.activation(res[:, HALF:D], ps[:, 1, :], ACT.Copy).then_inc(out_ev, 1)

            def final_std(b):
                wait_alone(eng, fin_var, b + 1)
                eng.activation(rstd2[:, :], rstd2[:, :], ACT.Sqrt).then_inc(fin_std, 1)

            def start_block(b, load=True):
                store(b - 2)
                evacuate(b - 1)
                if load:
                    wait_alone(eng, taken, b + 1)
                    load_next(b + 1)

            for s in range(8):
                a1(0, s)
            eng.wait_ge(dec_ready, 1)
            with eng.Fori(0, CT) as c:
                for s in range(4):
                    a2_step(0, c, s)
            for s in range(8):
                a3(0, s)
            with eng.Fori(0, QT // 8) as jj:
                for s in range(8):
                    a4(0, jj, s)
            eng.wait_ge(x1_stored, 16)
            load_next(0)
            with eng.Fori(0, LEAD) as g:
                softmax_exp(g)

            def head(g, phase=None, step=0, chosen=True):
                for c in range(2):
                    gelu(g, c)
                    if phase is not None:
                        phase(step + c)
                    if chosen and c == 0:
                        softmax_exp(g + LEAD)

            def channel_tile(c):
                for k in range(2):
                    head(c * 2 + (4 + k), lambda s: a2_step(1, c, s), 2 * k)

            eng.wait_ge(taken, 1)
            load_next(1)
            eng.wait_ge(kept, 2)
            for k in range(4):
                head(k, lambda s: a1(1, s), 2 * k)
            with eng.Fori(0, 2) as c:
                channel_tile(c)
            evacuate(0)
            eng.wait_ge(taken, 2)
            load_next(2)
            with eng.Fori(2, 6) as c:
                channel_tile(c)
            final_std(0)
            start_block(2)
            with eng.Fori(6, 8) as c:
                channel_tile(c)
            for k in range(4):
                head(20 + k, lambda s: a3(1, s), 2 * k)
            final_std(1)
            eng.wait_ge(x1_stored, 32)
            start_block(3)
            for k in range(8):
                head(24 + k, lambda s: a4(1, k // 4, s), 2 * (k % 4), chosen=24 + k + LEAD < NG // 2)
            final_std(2)
            with eng.Fori(NG // 2, NG // 2 + LEAD) as g:
                softmax_exp(g)

            with eng.Fori(NBLK // 2, NBLK - 1) as b:
                start_block(b)
                with eng.Fori(0, HEADS) as hd:
                    head(b * HEADS + hd)
                final_std(b - 1)
            start_block(NBLK - 1, load=False)
            with eng.Fori(NG - HEADS, NG - LEAD) as g:
                head(g)
            with eng.Fori(NG - LEAD, NG) as g:
                head(g, chosen=False)
            final_std(NBLK - 2)
            store(NBLK - 2)
            evacuate(NBLK - 1)
            final_std(NBLK - 1)
            store(NBLK - 1)

        @block.tensor
        def _(eng):
            eng.sem_inc(v_used, RING)
            eng.sem_inc(mix_mm, 1)

            def project(bank, w, rhs, done):
                for k in range(KT):
                    mm = eng.matmul(ps[:, bank, :], w[:, k, :], rhs[:, k, :],
                                    start=(k == 0), stop=(k == KT - 1))
                mm.then_inc(done, 1)

            def token_rows(bank, lhs, b, n0, done):
                for k in range(KT):
                    if b == 0 and k % 2 == 0:
                        eng.wait_ge(w_in[k // 2], 16 * (n0 + 1))
                    mm = eng.matmul(ps[:, bank, :], lhs(k, b), wrow(k), start=(k == 0), stop=(k == KT - 1))
                mm.then_inc(done, 1)

            SLOT = 2 + CT + 2 + QT // 4

            def a1(h, step):
                if step == 0:
                    eng.wait_ge(xt_in, 16 * (h + 1))
                for n in ((0, 1), (2,), (3,), (4,), (5,), (6,), (7,), ())[step]:
                    if n >= 2:
                        eng.wait_ge(v_gelu, 2 * BPH * h + n - 1)
                    token_rows(V_BANK + n % 2, lambda k, b: xt[:, k, b * P:(b + 1) * P], n % BPH,
                               SLOT * h + n // BPH, v_mm)
                if step == 7:
                    eng.wait_ge(v_gelu, 2 * BPH * (h + 1))

            def a2_step(h, c, step):
                n = c + (CT * h + 1)
                loaded = lambda j: eng.wait_ge(w_in[j], c * 16 + 16 * (SLOT * h + 3 if j < 4 else CT * h + 1))
                if step == 0:
                    eng.wait_ge(ri_ev, n)
                    loaded(0)
                    project(XA, wtile(0), xt, xa_mm)
                    loaded(1)
                    project(GA, wtile(1), xt, ga_mm)
                if step == 1:
                    eng.wait_ge(u_ev, n)
                    loaded(2)
                    project(U, wtile(2), xt, u_mm)
                    eng.wait_ge(g_a_ev, n)
                    loaded(3)
                    project(G_A, wtile(3), xt, g_a_mm)
                if step == 2:
                    rg = w_slot[4][:, TILE:].rearrange("p (a c) -> p a c", a=2)
                    loaded(4)
                    eng.wait_ge(xc_ready, n)
                    eng.wait_ge(ga_ev, n + 1)
                    eng.matmul(ps[:, R, :], rg[:, 0, :], xc[:, :], start=True, stop=True)
                    eng.matmul(ps[:, I, :], rg[:, 1, :], xc[:, :], start=True, stop=True).then_inc(ri_mm, 1)
                    eng.wait_ge(st_ready, n)
                    eng.wait_ge(mix_ev, n)
                    for b in range(BPH):
                        mm = eng.matmul(ps[:, MIX, b * P:(b + 1) * P], v_st[:, b, :],
                                        ws[:, bass.ds(c, 1), :].rearrange("p a t -> p (a t)"),
                                        start=True, stop=True)
                    mm.then_inc(mix_mm, 1)
                    eng.wait_ge(g_b_ev, n)
                    project(G_B, wtile(4), xt, g_b_mm)

            def a3(h, step):
                if step == 0:
                    eng.wait_ge(y_done, CT * (h + 1) + 1)
                if step < 4:
                    for n in (2 * step, 2 * step + 1):
                        if n >= 2:
                            eng.wait_ge(o_ev, 2 * BPH * h + n - 1)
                        token_rows(O_BANK + n % 2, lambda k, b: v_tok[:, b, k * P:(k + 1) * P], n % BPH,
                                   SLOT * h + 2 + CT + n // BPH, o_mm)
                if step in (4, 5):
                    for b in (2 * step - 8, 2 * step - 7):
                        eng.wait_ge(x1_ready, BPH * h + b + 1)
                        if b >= 2:
                            eng.wait_ge(t_ev, 2 * (BPH * h + b - 1))
                        for j in range(2):
                            for k in range(4):
                                mm = eng.transpose(ps[:, 2 + 4 * (b % 2) + j, k * P:(k + 1) * P],
                                                   x1[:, b, (4 * j + k) * P:(4 * j + k + 1) * P], ident[:, :])
                            mm.then_inc(t_mm, 1)

            def a4(h, jj, step):
                if step == 0:
                    eng.wait_ge(t_ev, 2 * BPH * (h + 1))
                for i in SC_STEPS[step]:
                    n = jj * 8 + (QT * h + i)
                    eng.wait_ge(q_ev, n + 3)
                    eng.wait_ge(sc_ev, n + 1)
                    for b in range(BPH):
                        mm = eng.matmul(ps[:, SC_BANK + i % 2, b * P:(b + 1) * P],
                                        q_s[i % 2][:, b * P:(b + 1) * P], w_slot[i % 4][:, TILE:QW],
                                        start=True, stop=True)
                    mm.then_inc(sc_mm, 1)
                for i in Q_STEPS[step]:
                    eng.wait_ge(w_in[i % 4], jj * 32 + 16 * (SLOT * h + 5 + CT + i // 4))
                    eng.wait_ge(q_ev, jj * 8 + (QT * h + i + 1))
                    project(Q_BANK + i % 2, wtile(i % 4), x1t, q_mm)

            def seed(b):
                wait_alone(eng, taken, b + 1)
                eng.wait_ge(out_ev, b + 1)
                for j in range(2):
                    eng.matmul(ps[:, j, :], ident_a[:, :], x1_now[:, j * HALF:(j + 1) * HALF],
                               start=True, stop=True)

            def head(g, phase=None, step=0):
                for c in range(2):
                    if phase is not None:
                        phase(step + c)
                    for s in range(RING):
                        eng.wait_ge(diag_ready, g * (2 * RING) + (c * RING + s + 1))
                        eng.wait_ge(v_in[s], g * 32 + 16 * (c + 1))
                        for j in range(2):
                            mm = eng.matmul(ps[:, j, :], diag[:, s, :], v_ring[s][:, j * HALF:(j + 1) * HALF],
                                            start=False, stop=False, skip_group_check=True)
                        mm.then_inc(v_used, 1)

            for s in range(8):
                a1(0, s)
            eng.wait_ge(masks, 1)
            with eng.Fori(0, CT) as c:
                for s in range(4):
                    a2_step(0, c, s)
            for s in range(8):
                a3(0, s)
            with eng.Fori(0, QT // 8) as jj:
                for s in range(8):
                    a4(0, jj, s)

            def channel_tile(c):
                for k in range(2):
                    head(c * 2 + (4 + k), lambda s: a2_step(1, c, s), 2 * k)

            seed(0)
            for k in range(4):
                head(k, lambda s: a1(1, s), 2 * k)
            eng.wait_ge(sc_ev, 2 + QT)
            with eng.Fori(0, 2) as c:
                channel_tile(c)
            seed(1)
            with eng.Fori(2, 6) as c:
                channel_tile(c)
            seed(2)
            with eng.Fori(6, 8) as c:
                channel_tile(c)
            for k in range(4):
                head(20 + k, lambda s: a3(1, s), 2 * k)
            seed(3)
            for k in range(8):
                head(24 + k, lambda s: a4(1, k // 4, s), 2 * (k % 4))

            with eng.Fori(NBLK // 2, NBLK) as b:
                seed(b)
                with eng.Fori(0, HEADS) as hd:
                    head(b * HEADS + hd)

        @block.vector
        def _(eng):
            eng.sem_inc(mix_ev, 1)
            eng.sem_inc(y_done, 1)
            eng.sem_inc(sc_ev, 2)
            eng.sem_inc(u_used, RING)
            eng.memset(halo[:, :, :], 0.0)
            eng.memset(h_last[:, :], 0.0)

            lam = chan[:, LAM, :]
            eng.wait_ge(const_in, 16 * 5)
            eng.tensor_scalar(sp[:, 5, :], lam, -1.0, None, ALU.mult)
            eng.drain()
            eng.tensor_tensor(sp[:, 0, :], lam, sp[:, 5, :], ALU.max).then_inc(lam_abs, 1)
            eng.wait_ge(lam_exp, 1)
            eng.tensor_scalar(sp[:, 2, :], sp[:, 1, :], 2.0, None, ALU.add)
            eng.drain()
            eng.reciprocal(sp[:, 2, :], sp[:, 2, :])
            eng.drain()
            eng.tensor_tensor(sp[:, 2, :], sp[:, 1, :], sp[:, 2, :], ALU.mult)
            eng.drain()
            eng.tensor_tensor(sp[:, 3, :], sp[:, 2, :], sp[:, 2, :], ALU.mult)
            terms = 9
            eng.drain()
            eng.tensor_scalar(sp[:, 4, :], sp[:, 3, :], 2.0 / (2 * terms + 1), 2.0 / (2 * terms - 1),
                              ALU.mult, ALU.add)
            for k in range(terms - 2, -1, -1):
                eng.drain()
                eng.tensor_tensor(sp[:, 4, :], sp[:, 4, :], sp[:, 3, :], ALU.mult)
                eng.drain()
                eng.tensor_scalar(sp[:, 4, :], sp[:, 4, :], 2.0 / (2 * k + 1), None, ALU.add)
            eng.drain()
            eng.tensor_tensor(sp[:, 4, :], sp[:, 4, :], sp[:, 2, :], ALU.mult)
            eng.tensor_scalar(sp[:, 5, :], sp[:, 5, :], 0.0, None, ALU.max)
            eng.drain()
            eng.tensor_tensor(sp[:, 4, :], sp[:, 4, :], sp[:, 5, :], ALU.add)
            eng.drain()
            eng.tensor_scalar(dec[:, 0, :], sp[:, 4, :], -LRU_C, None, ALU.mult)
            eng.tensor_scalar(dec[:, 1, :], sp[:, 4, :], LRU_C, None, ALU.mult).then_inc(dec_ready, 1)
            eng.wait_ge(masks, 1)
            eng.tensor_scalar(ident_a[:, :], ident[:, :], ALPHA, None, ALU.mult)

            def variance(lo, hi):
                eng.drain()
                for b in range(lo, hi):
                    eng.bn_aggr(mv[:, b, :], stats[:, b, :, :])
                eng.drain()
                eng.tensor_scalar(rstd[:, lo:hi], mv[:, lo:hi, 1], EPS, None, ALU.add).then_inc(var_ready, 1)

            def inverse(lo, hi, n):
                eng.drain()
                eng.wait_ge(std_ready, n)
                eng.reciprocal(rstd[:, lo:hi], rstd[:, lo:hi])
                eng.drain()

            def normalise(data, mean, inv, gb):
                eng.tensor_scalar(data, data, mean, inv, ALU.subtract, ALU.mult)
                eng.drain()
                eng.tensor_tensor(data, data, gb[:, 0, :], ALU.mult)
                eng.drain()
                return eng.tensor_tensor(data, data, gb[:, 1, :], ALU.add)

            def convolve(h, c):
                n = c + (CT * h + 1)
                ch = lambda row: chan[:, row, bass.ds(c, 1)]
                hal = halo[:, bass.ds(c, 1), :].rearrange("p a k -> p (a k)")
                eng.drain()
                eng.tensor_copy(xa[:, 0:CONV - 1], hal)
                eng.drain()
                eng.wait_ge(xa_ev, n + 1)
                eng.tensor_scalar(xc[:, :], xa[:, CONV - 1:], ch(CW + CONV - 1), ch(CB), ALU.mult, ALU.add)
                for k in range(CONV - 1):
                    eng.drain()
                    step = eng.scalar_tensor_tensor(out=xc[:, :], in0=xa[:, k:k + HALF], scalar=ch(CW + k),
                                                    in1=xc[:, :], op0=ALU.mult, op1=ALU.add)
                step.then_inc(xc_ready, 1)
                eng.tensor_copy(hal, xa[:, HALF:HALF + CONV - 1])

            def recur_and_merge(h, c):
                n = c + (CT * h + 1)
                eng.drain()
                eng.wait_ge(decay, n)
                eng.scalar_tensor_tensor(out=rr[:, :], in0=a2[:, :], scalar=1.0, in1=rr[:, :],
                                         op0=ALU.add, op1=ALU.mult).then_inc(one_less, 1)
                eng.tensor_tensor(ii[:, :], ii[:, :], xc[:, :], ALU.mult)
                eng.drain()
                eng.wait_ge(root, n)
                eng.tensor_tensor(ii[:, :], ii[:, :], rr[:, :], ALU.mult)
                eng.drain()
                eng.tensor_tensor_scan(a2[:, :], aa[:, :], ii[:, :], h_last[:, bass.ds(c, 1)],
                                       ALU.mult, ALU.add)
                eng.drain()
                eng.tensor_copy(h_last[:, bass.ds(c, 1)], a2[:, HALF - 1:HALF])
                eng.tensor_tensor(gg[:, :], gg[:, :], a2[:, :], ALU.mult)
                eng.drain()
                eng.wait_ge(g_a_ev, n + 1)
                eng.tensor_tensor(gg[:, :], gg[:, :], s_a[:, :], ALU.mult)
                eng.wait_ge(mix_mm, n + 1)
                bias = bs_b[:, bass.ds(c, 1), :].to_broadcast([P, BPH, P])
                eng.tensor_tensor(xc[:, :].rearrange("p (b t) -> p b t", b=BPH),
                                  ps[:, MIX, :].rearrange("p (b t) -> p b t", b=BPH), bias,
                                  ALU.add).then_inc(mix_ev, 1)
                eng.drain()
                eng.tensor_tensor(xc[:, :], xc[:, :], gu[:, :], ALU.mult)
                eng.drain()
                eng.wait_ge(g_b_ev, n + 1)
                eng.tensor_tensor(xc[:, :], xc[:, :], s_b[:, :], ALU.mult)
                eng.drain()
                eng.tensor_tensor(v_tok[:, :, bass.ds(c * P, P)],
                                  gg[:, :].rearrange("p (b t) -> p b t", b=BPH),
                                  xc[:, :].rearrange("p (b t) -> p b t", b=BPH), ALU.add).then_inc(y_done, 1)

            def top_keys(h, jj, i):
                n = jj * 8 + (QT * h + i)
                score = lambda b: ps[:, SC_BANK + i % 2, b * P:(b + 1) * P]
                wait_alone(eng, sc_mm, n + 1)
                eng.drain()
                for b in range(BPH):
                    eng.max(top_st[:, b, i, 0:8], score(b))
                eng.drain()
                for b in range(BPH):
                    eng.match_replace(knock[:, b, :], top_st[:, b, i, 0:8], score(b), LOWEST)
                for b in range(BPH):
                    eng.max_index(key_st[:, b, i, 0:8], top_st[:, b, i, 0:8], score(b))
                eng.drain()
                for b in range(BPH):
                    eng.max(top_st[:, b, i, 8:16], knock[:, b, :])
                eng.drain()
                for b in range(BPH):
                    last = eng.max_index(key_st[:, b, i, 8:16], top_st[:, b, i, 8:16], knock[:, b, :])
                last.then_inc(sc_ev, 1)

            def a1(h, step):
                for n in ((), (0, 1), (2,), (3,), (4,), (5,), (6,), (7,))[step]:
                    half, b = divmod(n, BPH)
                    eng.wait_ge(v_gelu, 2 * BPH * h + n + 1)
                    eng.bn_stats(stats[:, b, half, :], v_tok[:, b, half * HALF:(half + 1) * HALF])
                if step == 7:
                    variance(0, BPH)
                    inverse(0, BPH, (BPH + 1) * h + 1)
                    eng.wait_ge(ln_in, 32 * (2 * h + 1))
                    for b in range(BPH):
                        last = normalise(v_tok[:, b, :], mv[:, b, 0:1], rstd[:, b:b + 1], ln_gb)
                    last.then_inc(v_norm, 1)
                    eng.drain()

            def a2_step(h, c, step):
                if step == 1:
                    convolve(h, c)
                if step == 3:
                    recur_and_merge(h, c)

            def a3(h, step):
                if step == 1:
                    eng.wait_ge(x_in, 16 * (h + 1))
                    eng.wait_ge(ln_in, 32 * (2 * h + 2))
                if 1 <= step <= 4:
                    for n in (2 * step - 2, 2 * step - 1):
                        half, b = divmod(n, BPH)
                        part = x1[:, b, half * HALF:(half + 1) * HALF]
                        eng.wait_ge(o_mm, 2 * BPH * h + n + 1)
                        eng.scalar_tensor_tensor(out=part, in0=part, scalar=ALPHA, in1=ps[:, O_BANK + n % 2, :],
                                                 op0=ALU.mult, op1=ALU.add).then_inc(o_ev, 1)
                        eng.drain()
                        eng.bn_stats(stats[:, b, half, :], part)
                        if half:
                            variance(b, b + 1)
                            inverse(b, b + 1, (BPH + 1) * h + 2 + b)
                            normalise(x1[:, b, :], mv[:, b, 0:1], rstd[:, b:b + 1], ln_gb
                                      ).then_inc(x1_ready, 1)

            def a4(h, jj, step):
                for i in (SC_STEPS[step - 1] if step else ()):
                    top_keys(h, jj, i)
                if step == 7:
                    eng.drain()
                    for dst, src in ((top_v, top_st), (top_i, key_st)):
                        for b in range(BPH):
                            last = eng.tensor_copy(
                                dst[:, bass.ds(jj * 4 + (BPH * h + b) * HEADS, 4), :, :].rearrange(
                                    "p g a k -> p (g a k)"), src[:, b, :, :].rearrange("p i k -> p (i k)"))
                    last.then_inc(kept, 1)
                    eng.drain()

            def select(g):
                val = top_v[:, bass.ds(g, 1), :, :].rearrange("p g a k -> p (g a) k")
                key = top_i[:, bass.ds(g, 1), :, :].rearrange("p g a k -> p (g a) k")
                grid = [P, TOPK, TOPK]
                eng.drain()
                eng.tensor_tensor(cand[:, :].rearrange("p (a b) -> p a b", a=TOPK),
                                  val[:, 0, :].unsqueeze(2).to_broadcast(grid),
                                  val[:, 1, :].unsqueeze(1).to_broadcast(grid), ALU.add)
                eng.drain()
                eng.max(best[:, 0:8], cand[:, :])
                eng.drain()
                eng.match_replace(cand2[:, :], best[:, 0:8], cand[:, :], LOWEST)
                eng.max_index(pos[:, 0:8], best[:, 0:8], cand[:, :])
                eng.drain()
                eng.max(best[:, 8:16], cand2[:, :])
                eng.drain()
                eng.max_index(pos[:, 8:16], best[:, 8:16], cand2[:, :])
                eng.tensor_scalar(less[:, :], best[:, :], best[:, 0:1], None, ALU.subtract
                                  ).then_inc(less_ready, 1)
                eng.drain()
                eng.tensor_scalar(pair[:, 0, :], pos[:, :], 4, None, ALU.logical_shift_right)
                eng.tensor_scalar(pair[:, 1, :], pos[:, :], TOPK - 1, None, ALU.bitwise_and)
                eng.drain()
                quad = [P, 2, TOPK, TOPK]
                eng.tensor_tensor(hot[:, :, :, :], pair[:, :, :].unsqueeze(3).to_broadcast(quad),
                                  iota[:, :].unsqueeze(1).unsqueeze(1).to_broadcast(quad), ALU.is_equal)
                eng.drain()
                eng.tensor_tensor(hot[:, :, :, :], hot[:, :, :, :],
                                  key.unsqueeze(2).to_broadcast(quad), ALU.mult)
                eng.drain()
                eng.tensor_reduce(picked[:, :, :], hot[:, :, :, :], AX_X, ALU.add)
                eng.drain()
                eng.scalar_tensor_tensor(out=ids[:, bass.ds(g, 1), :].rearrange("p g k -> p (g k)"),
                                         in0=picked[:, 0, :], scalar=float(NKEY), in1=picked[:, 1, :],
                                         op0=ALU.mult, op1=ALU.add).then_inc(ids_ready, 1)

            def gate(g):
                eng.drain()
                eng.wait_ge(exp_done, g + 1)
                eng.tensor_reduce(tot[:, 0:1], expo[:, :], AX_X, ALU.add)
                eng.drain()
                eng.reciprocal(tot[:, 1:2], tot[:, 0:1])
                eng.drain()
                eng.tensor_scalar(gates[:, bass.ds(g * TOPK, TOPK)], expo[:, :], tot[:, 1:2], None, ALU.mult)
                eng.drain()

            def dots(g, c):
                for s in range(RING):
                    eng.wait_ge(u_in[s], g * 32 + 16 * (c + 1))
                    eng.tensor_tensor_reduce(u_ring[s], u_ring[s], x1_now[:, :], 1.0, 0.0, ALU.mult, ALU.add,
                                             hdot[:, c, s:s + 1]).then_inc(u_used, 1)

            def diagonals(g, c):
                wait_alone(eng, gelu_done, g * 2 + (c + 1))
                eng.drain()
                eng.tensor_tensor(wact[:, :], hact[:, c, :], gates[:, bass.ds(g * TOPK + c * RING, RING)],
                                  ALU.mult)
                eng.drain()
                for s in range(RING):
                    eng.wait_ge(v_used, g * (2 * RING) + (c * RING + s + 1))
                    eng.tensor_scalar(diag[:, s, :], ident[:, :], wact[:, s:s + 1], None, ALU.mult
                                      ).then_inc(diag_ready, 1)

            def take_block(b):
                eng.drain()
                eng.wait_ge(next_in, b * 16 + 16)
                eng.tensor_copy(x1_now[:, :], x1_next[:, :]).then_inc(taken, 1)
                eng.drain()

            def finish(b):
                wait_alone(eng, out_ev, b + 2)
                eng.drain()
                for j in range(2):
                    eng.bn_stats(stats2[:, j, :], res[:, j * HALF:(j + 1) * HALF])
                eng.drain()
                eng.bn_aggr(mv2[:, :], stats2[:, :, :])
                eng.drain()
                eng.tensor_scalar(rstd2[:, :], mv2[:, 1:2], EPS, None, ALU.add).then_inc(fin_var, 1)
                eng.drain()
                eng.wait_ge(fin_std, b + 1)
                eng.reciprocal(rstd2[:, :], rstd2[:, :])
                eng.drain()
                normalise(res[:, :], mv2[:, 0:1], rstd2[:, 0:1], ln2_gb).then_inc(fin, 1)

            for s in range(8):
                a1(0, s)
            with eng.Fori(0, CT) as c:
                for s in range(4):
                    a2_step(0, c, s)
            for s in range(8):
                a3(0, s)
            with eng.Fori(0, QT // 8) as jj:
                for s in range(8):
                    a4(0, jj, s)
            with eng.Fori(0, LEAD) as g:
                select(g)
                gate(g)

            def head(g, phase=None, step=0, chosen=True, first=False):
                dots(g, 0)
                if not first:
                    diagonals(g - 1, 1)
                if phase is not None:
                    phase(step)
                if chosen:
                    select(g + LEAD)
                dots(g, 1)
                diagonals(g, 0)
                if phase is not None:
                    phase(step + 1)
                if chosen:
                    gate(g + LEAD)

            def channel_tile(c):
                for k in range(2):
                    head(c * 2 + (4 + k), lambda s: a2_step(1, c, s), 2 * k)

            take_block(0)
            for k in range(4):
                head(k, lambda s: a1(1, s), 2 * k, first=(k == 0))
            with eng.Fori(0, 2) as c:
                channel_tile(c)
            take_block(1)
            with eng.Fori(2, 6) as c:
                channel_tile(c)
            finish(0)
            take_block(2)
            with eng.Fori(6, 8) as c:
                channel_tile(c)
            for k in range(4):
                head(20 + k, lambda s: a3(1, s), 2 * k)
            finish(1)
            take_block(3)
            for k in range(8):
                head(24 + k, lambda s: a4(1, k // 4, s), 2 * (k % 4), chosen=24 + k + LEAD < NG // 2)
            finish(2)
            with eng.Fori(NG // 2, NG // 2 + LEAD) as g:
                select(g)
                gate(g)

            with eng.Fori(NBLK // 2, NBLK - 1) as b:
                take_block(b)
                with eng.Fori(0, HEADS) as hd:
                    head(b * HEADS + hd)
                finish(b - 1)
            take_block(NBLK - 1)
            with eng.Fori(NG - HEADS, NG - LEAD) as g:
                head(g)
            with eng.Fori(NG - LEAD, NG) as g:
                head(g, chosen=False)
            diagonals(NG - 1, 1)
            finish(NBLK - 2)
            finish(NBLK - 1)


def kernel(**inputs):
    import numpy as np
    import concourse.bacc as bacc
    from concourse.bass_utils import run_bass_kernel_spmd

    a = {k: np.asarray(v) for k, v in inputs.items()}

    def tiles(w):
        return w.reshape(KT, P, -1, P).transpose(2, 1, 0, 3)

    def halves(w):
        return w.reshape(KT, P, 2, HALF).transpose(2, 1, 0, 3).reshape(2, P, KT * HALF)

    w_in = a["w_in"][0]
    wt = tiles(w_in)
    mix = [wt[CT * j:CT * (j + 1)].reshape(CT, P, TILE) for j in (0, 1, 2, 4, 5)]
    keys_t = a["peer_sub_keys"][0].reshape(QT, NKEY, P).transpose(0, 2, 1)
    cols = np.concatenate([a["conv_w"][0], a["conv_b"], a["rg_b_a"], a["rg_b_x"], a["rg_lambda"],
                           a["b_gate"][0]])
    arrays = {
        "x": a["x"][0],
        "x_t": a["x"][0].T.reshape(KT, P, NHALF, HALF).transpose(2, 1, 0, 3).reshape(NHALF, P, KT * HALF),
        "w_mix": np.stack(mix[:4]),
        "w_gb": np.concatenate([mix[4], a["rg_w_a"][0], a["rg_w_x"][0]], axis=2),
        "w_v": halves(w_in[:, 3 * D:4 * D]),
        "w_out": halves(a["w_out"][0]),
        "w_q": np.concatenate([tiles(a["peer_wq"][0]).reshape(QT, P, TILE), keys_t], axis=2),
        "ws_t": a["gm_ws"][0].transpose(2, 0, 1),
        "bs": a["gm_bs"][0].reshape(-1),
        "chan": cols.reshape(NCHAN, CT, P).transpose(2, 0, 1),
        "ln": np.stack([np.stack([a[g][0], a[b][0]]) for g, b in
                        (("gm_ln_g", "gm_ln_b"), ("ln1_g", "ln1_b"), ("ln2_g", "ln2_b"))]),
        "peer_u": a["peer_u"][0],
        "peer_v": a["peer_v"][0],
    }
    arrays = {f"{k}_dram": np.ascontiguousarray(v) for k, v in arrays.items()}
    nc = bacc.Bacc("TRN2", target_bir_lowering=False, num_devices=1)
    args = [nc.dram_tensor(k, v.shape, mybir.dt.from_np(v.dtype), kind="ExternalInput").ap()
            for k, v in arrays.items()]
    out = nc.dram_tensor("out_dram", (T, D), F32, kind="ExternalOutput").ap()
    x1_d = nc.dram_tensor("x1_scratch", (T, D), F32, kind="Internal").ap()
    build(nc, *args, x1_d, out)
    r = run_bass_kernel_spmd(nc, [arrays], core_ids=[0])
    return r.results[0]["out_dram"].reshape(1, T, D)
```

```python
from contextlib import ExitStack

import concourse.bass as bass
from concourse import mybir

ALU = mybir.AluOpType
ACT = mybir.ActivationFunctionType
F32 = mybir.dt.float32
F32R = mybir.dt.float32r
U32 = mybir.dt.uint32
U16 = mybir.dt.uint16
AX_X = mybir.AxisListType.X

P = 128
D = 1024
T = 1024
KT = D // P
CT = D // P
HALF = 512
NHALF = T // HALF
BPH = HALF // P
NBLK = T // P
HEADS = 8
NKEY = 128
TOPK = 16
QT = 2 * HEADS
NG = NBLK * HEADS
RING = 8
LEAD = 1
CONV = 4
LRU_C = 8.0
ALPHA = 2.0 ** 0.25
EPS = 1e-5
LOWEST = -3.0e38
TILE = KT * P
QW = TILE + P
GBW = TILE + 2 * P
CW, CB, BA, BX, LAM, BGA, BGB = 0, 4, 5, 6, 7, 8, 9
NCHAN = 10
XA, GA, R, I, U, G_A, MIX, G_B = 2, 3, 2, 3, 4, 5, 6, 7
TOKEN_BANKS = (2, 3, 4, 5, 6, 7, 0, 1)
V_BANK, O_BANK, Q_BANK, SC_BANK = 6, 4, 2, 4
A1_STEPS = ((0, 1), (2, 3), (4,), (5, 6), (7,), ())
A1_LATER = ((),) + A1_STEPS[:-1]
A4_STEPS = QT + 2
A4_AHEAD = 7
A4_FIRST_MM = ((0, 1, 2, 3, 4), (5, 6), (7,), (8,), (9, 10), (11,), (12, 13), (14,), (15,), (16,))
A4_FIRST = ((0, 1, 2, 3), (4, 5), (6, 7), (8,), (9,), (10, 11), (12,), (13, 14), (15,), (16,), (17,))
A1_FROM = 2 * HEADS - len(A1_STEPS)
assert max(A4_FIRST_MM[A1_FROM - 1]) == QT


def build(nc, x, x_t, w_mix, w_gb, w_v, w_out, w_q, ws_t, bs, chan_d, ln_d, peer_u, peer_v, x1_d, out):
    with ExitStack() as ctx:
        def sb(name, shape, dt=F32):
            return ctx.enter_context(nc.sbuf_tensor(name, shape, dt))

        def sem(name):
            return ctx.enter_context(nc.semaphore(name))

        ring_at = -(-nc.sbuf_base // 32) * 32
        u_area, v_rows = sb("u_area", [P, RING, D]), sb("v_rows", [P, RING, D])
        x1_next, x1_now = sb("x1_next", [P, D]), sb("x1_now", [P, D])
        def part(name, shape, offset):
            return nc.alloc_sbuf_tensor_at(name, shape, F32R, offset=ring_at + offset)

        x_parts = [part(f"x_{n}", [P, KT, HALF], 4 * KT * HALF * i) for i, n in enumerate(("high", "low"))]
        y_parts = [part(f"y_{n}", [P, BPH, D], 4 * BPH * D * i) for i, n in enumerate(("high", "low"))]
        w_parts = [[part(f"w{j}_{n}", [P, TILE], 4 * (2 * KT * HALF + (2 * j + i) * TILE))
                    for i, n in enumerate(("high", "low"))] for j in range(5)]
        w_area = sb("w_area", [P, 4 * QW + GBW])
        w_slot = [w_area[:, j * QW:(j + 1) * QW] for j in range(4)] + [w_area[:, 4 * QW:]]
        x_area = sb("x_area", [P, KT * HALF])
        xt = x_area[:, :].rearrange("p (k t) -> p k t", k=KT)
        x1 = x_area[:, :].rearrange("p (b d) -> p b d", b=BPH)
        v_area = sb("v_area", [P, KT * HALF])
        v_tok = v_area[:, :].rearrange("p (b c) -> p b c", b=BPH)
        x1t = v_area[:, :].rearrange("p (k t) -> p k t", k=KT)
        u_ring = [u_area[:, s, :] for s in range(RING)]
        v_ring = [v_rows[:, s, :] for s in range(RING)]
        diag = sb("diag", [P, RING, P])
        res = sb("res", [P, D])

        ws = sb("ws", [P, CT, P])
        bs_b = sb("bs_b", [P, CT, P])
        ln_gb = sb("ln_gb", [P, 2, D])
        ln2_gb = sb("ln2_gb", [P, 2, D])
        chan = sb("chan", [P, NCHAN, CT])
        xa = sb("xa", [P, CONV - 1 + HALF])
        halo = sb("halo", [P, CT, CONV - 1])
        h_last = sb("h_last", [P, CT])
        xc, gg, rr, ii, aa, a2, gu, s_a, s_b = (
            sb(n, [P, HALF]) for n in ("xc", "gg", "rr", "ii", "aa", "a2", "gu", "s_a", "s_b"))
        v_st = sb("v_st", [P, BPH, P])
        q_s = [gg, rr]
        knock = ii[:, :].rearrange("p (b n) -> p b n", b=BPH)
        first_q = s_a[:, 0:2 * P].rearrange("p (i t) -> p i t", i=2)
        first_knock = s_b[:, 0:P]
        top_v = sb("top_v", [P, NG, 2, TOPK])
        top_i = sb("top_i", [P, NG, 2, TOPK], U16)
        ids = sb("ids", [P, NG, TOPK], U16)
        gates = sb("gates", [P, NG * TOPK])
        id_now = sb("id_now", [P, 2, TOPK], U32)
        cand = sb("cand", [P, TOPK * TOPK])
        cand2 = sb("cand2", [P, TOPK * TOPK])
        best = sb("best", [P, TOPK])
        pos = sb("pos", [P, TOPK], U32)
        pair = sb("pair", [P, 2, TOPK], U32)
        hot = sb("hot", [P, 2, TOPK, TOPK])
        picked = sb("picked", [P, 2, TOPK])
        less = sb("less", [P, TOPK])
        expo = sb("expo", [P, TOPK])
        tot = sb("tot", [P, 2])
        hdot = sb("hdot", [P, 2, RING])
        hact = sb("hact", [P, 2, RING])
        wact = sb("wact", [P, RING])
        ident = sb("ident", [P, P])
        ident_a = sb("ident_a", [P, P])
        iota = sb("iota", [P, TOPK], U32)
        stats = sb("stats", [P, BPH, 2, 6])
        mv = sb("mv", [P, BPH, 2])
        rstd = sb("rstd", [P, BPH])
        stats2, mv2, rstd2 = sb("stats2", [P, 2, 6]), sb("mv2", [P, 2]), sb("rstd2", [P, 1])
        sp = sb("sp", [P, 6, CT])
        dec = sb("dec", [P, 2, CT])
        ps = ctx.enter_context(nc.psum_tensor("ps", [P, 8, HALF], F32))

        const_in, x_in, ln_in = sem("const_in"), sem("x_in"), sem("ln_in")
        xt_in = [sem(f"xt_in{j}") for j in range(4)]
        w_in = [sem(f"w_in{j}") for j in range(5)]
        masks = sem("masks")
        lam_abs, lam_exp, dec_ready = sem("lam_abs"), sem("lam_exp"), sem("dec_ready")
        x_high, x_split, w_high, w_split = sem("x_high"), sem("x_split"), sem("w_high"), sem("w_split")
        y_high, y_split = sem("y_high"), sem("y_split")
        first_q_mm, first_q_ev, first_sc_mm = sem("first_q_mm"), sem("first_q_ev"), sem("first_sc_mm")
        w_half_used = sem("w_half_used")
        v_mm, v_gelu, v_norm = sem("v_mm"), sem("v_gelu"), sem("v_norm")
        xa_mm, ga_mm, ri_mm, u_mm, mix_mm, g_a_mm, g_b_mm = (
            sem(n) for n in ("xa_mm", "ga_mm", "ri_mm", "u_mm", "mix_mm", "g_a_mm", "g_b_mm"))
        xa_ev, ga_ev, ri_ev, u_ev, mix_ev, g_a_ev, g_b_ev = (
            sem(n) for n in ("xa_ev", "ga_ev", "ri_ev", "u_ev", "mix_ev", "g_a_ev", "g_b_ev"))
        x1_stored = sem("x1_stored")
        xc_ready, decay = sem("xc_ready"), sem("decay")
        one_less, root = sem("one_less"), sem("root")
        var_ready, std_ready = sem("var_ready"), sem("std_ready")
        y_done = sem("y_done")
        st_ready = sem("st_ready")
        o_mm, o_ev, x1_ready, t_mm, t_ev = (
            sem(n) for n in ("o_mm", "o_ev", "x1_ready", "t_mm", "t_ev"))
        q_mm, sc_mm = sem("q_mm"), sem("sc_mm")
        q_ev, sc_ev = sem("q_ev"), sem("sc_ev")
        ids_ready, less_ready, exp_done = sem("ids_ready"), sem("less_ready"), sem("exp_done")
        id_copied = sem("id_copied")
        u_in = [sem(f"u_in{s}") for s in range(RING)]
        v_in = [sem(f"v_in{s}") for s in range(RING)]
        u_used, v_used = sem("u_used"), sem("v_used")
        gelu_done, diag_ready = sem("gelu_done"), sem("diag_ready")
        out_ev = sem("out_ev")
        next_in, taken = sem("next_in"), sem("taken")
        fin_var, fin_std, fin = sem("fin_var"), sem("fin_std"), sem("fin")
        stored = sem("stored")
        tick = sem("tick")

        def wait_alone(eng, s, value):
            eng.wait_ge(s, value)
            eng.sem_inc(tick, 1)

        def tile_of(h, t):
            return (2, 3, 0, 1)[t] if h == 0 and t < 4 else t

        def first_block_of(h, t):
            return 1 if h == 0 and tile_of(h, t) < 2 else 0

        def wtile(j):
            return w_slot[j][:, 0:TILE].rearrange("p (k c) -> p k c", k=KT)

        def wrow(k):
            return w_slot[k // 2][:, (k % 2) * HALF:(k % 2 + 1) * HALF]

        A2_SPLIT = 8
        A3_SPLIT = A2_SPLIT + 5 * CT
        Y_PIECES = ((0, 2), (2, 4), (4, 6), (6, 7), (7, 8))
        PRODUCTS = ((0, 0), (0, 1), (1, 0))

        block = ctx.enter_context(nc.Block())

        @block.sync
        def _(eng):
            def load_ln(dst, n, landed):
                for j in range(2):
                    eng.dma_start(dst[:, j, :], ln_d[n, j].partition_broadcast(P)).then_inc(landed, 16)

            def load_half(w, half):
                for j in range(4):
                    eng.dma_start(w_slot[j][:, 0:TILE], w[half][:, j * TILE:(j + 1) * TILE]
                                  ).then_inc(w_in[j], 16)

            def load_mix(c, j):
                src = w_mix[j] if j < 4 else w_gb
                eng.dma_start(w_slot[j][:, 0:TILE if j < 4 else GBW],
                              src[bass.ds(c, 1)].rearrange("a p n -> (a p) n")).then_inc(w_in[j], 16)

            for h in range(NHALF):
                if h:
                    eng.wait_ge(t_mm, 2 * BPH * h)
                    eng.wait_ge(x1_stored, 16 * h)
                    eng.wait_ge(taken, 1)
                for j in range(4):
                    eng.dma_start(x_area[:, j * TILE:(j + 1) * TILE], x_t[h][:, j * TILE:(j + 1) * TILE]
                                  ).then_inc(xt_in[j], 16)
                    if h:
                        eng.wait_ge(sc_mm, QT * h - 3 + j)
                    eng.dma_start(w_slot[j][:, 0:TILE], w_v[0][:, j * TILE:(j + 1) * TILE]
                                  ).then_inc(w_in[j], 16)
                if h == 0:
                    eng.dma_start(chan[:, :, :], chan_d).then_inc(const_in, 16)
                    eng.dma_start(ws[:, :, :], ws_t).then_inc(const_in, 16)
                    eng.dma_start(bs_b[:, :, :].rearrange("p c t -> p (c t)"),
                                  bs.partition_broadcast(P)).then_inc(const_in, 16)
                    load_ln(ln_gb, 0, ln_in)
                    load_ln(ln2_gb, 2, const_in)
                if h == 0:
                    for j in range(4):
                        eng.wait_ge(w_split, j + 1)
                        eng.dma_start(w_slot[j][:, 0:TILE], w_v[1][:, j * TILE:(j + 1) * TILE]
                                      ).then_inc(w_in[j], 16)
                    for j in range(4):
                        eng.wait_ge(w_split, 4 + j + 1)
                        load_mix(0, j)
                    load_mix(0, 4)
                    with eng.Fori(1, CT) as c:
                        for j in range(5):
                            eng.wait_ge(w_split, c * 5 + (A2_SPLIT - 5 + j + 1))
                            if j == 4:
                                eng.wait_ge(ri_mm, c)
                            load_mix(c, j)
                else:
                    eng.wait_ge(v_mm, 2 * BPH * h + BPH)
                    load_half(w_v, 1)
                    load_mix(0, 4)
                    eng.wait_ge(v_mm, 2 * BPH * (h + 1))
                    for j in range(4):
                        load_mix(0, j)
                    with eng.Fori(1, CT) as c:
                        for j, used in enumerate((xa_mm, ga_mm, u_mm, g_a_mm, g_b_mm)):
                            eng.wait_ge(used, c + CT * h)
                            load_mix(c, j)
                eng.wait_ge(v_norm, h + 1)
                load_ln(ln_gb, 1, ln_in)
                if h:
                    eng.wait_ge(g_a_mm, CT * (h + 1))
                for j in range(4):
                    if h == 0:
                        eng.wait_ge(w_split, A3_SPLIT - 5 + j + 1)
                    eng.dma_start(w_slot[j][:, 0:TILE], w_out[0][:, j * TILE:(j + 1) * TILE]
                                  ).then_inc(w_in[j], 16)
                eng.wait_ge(g_b_mm, CT * (h + 1))
                eng.dma_start(x1, x[h * HALF:(h + 1) * HALF, :].rearrange("(b p) d -> p b d", p=P)
                              ).then_inc(x_in, 16)
                if h:
                    eng.wait_ge(o_mm, 2 * BPH * h + BPH)
                for j in range(4):
                    if h == 0:
                        eng.wait_ge(w_split, A3_SPLIT + j + 1)
                    eng.dma_start(w_slot[j][:, 0:TILE], w_out[1][:, j * TILE:(j + 1) * TILE]
                                  ).then_inc(w_in[j], 16)
                if h:
                    eng.wait_ge(o_mm, 2 * BPH * (h + 1))
                for j in ((2, 3, 0, 1) if h == 0 else range(4)):
                    if h == 0:
                        eng.wait_ge(w_split, A3_SPLIT + 4 + j + 1)
                    eng.dma_start(w_slot[j], w_q[tile_of(h, j)]).then_inc(w_in[j], 16)
                eng.wait_ge(x1_ready, BPH * (h + 1))
                eng.dma_start(x1_d[h * HALF:(h + 1) * HALF, :].rearrange("(b p) d -> p b d", p=P),
                              x1).then_inc(x1_stored, 16)
                if h < NHALF - 1:
                    load_ln(ln_gb, 0, ln_in)
                with eng.Fori(1, QT // 4) as i4:
                    for j in range(4):
                        eng.wait_ge(sc_mm, i4 * 4 + (QT * h + j - 3))
                        eng.dma_start(w_slot[j], w_q[bass.ds(i4 * 4 + j, 1)].rearrange(
                            "a p n -> (a p) n")).then_inc(w_in[j], 16)

        @block.gpsimd
        def _(eng):
            eng.memset(ident[:, :], 0.0)
            eng.iota(iota[:, :], pattern=[[1, TOPK]], base=0, channel_multiplier=0)
            eng.drain()
            eng.affine_select(out=ident[:, :], in_=ident[:, :], compare_op=ALU.not_equal, fill=1.0,
                              base=0, pattern=[[-1, P]], channel_multiplier=1)
            eng.wait_ge(const_in, 16 * 5)
            eng.affine_select(out=ws[:, :, :], in_=ws[:, :, :], compare_op=ALU.is_ge, fill=0.0,
                              base=0, pattern=[[0, CT], [1, P]], channel_multiplier=-1
                              ).then_inc(masks, 1)

            def gather(ring, landed, table, used, par, g, c, s):
                wait_alone(eng, used, g * (2 * RING) + (c * RING + s + 1))
                eng.indirect_dma_start(ring[s], None, table, bass.IndirectOffsetOnAxis(
                    ap=id_now[:, par, c * RING + s:c * RING + s + 1], axis=0)).then_inc(landed[s], 16)

            def gather_u(par, g, c):
                for s in range(RING):
                    gather(u_ring, u_in, peer_u, u_used, par, g, c, s)

            def gather_v(par, g, c):
                for s in range(RING):
                    gather(v_ring, v_in, peer_v, v_used, par, g, c, s)

            def head(par, g, first=False):
                wait_alone(eng, ids_ready, g + 1)
                eng.tensor_copy(id_now[:, par, :], ids[:, bass.ds(g, 1), :].rearrange(
                    "p a k -> p (a k)")).then_inc(id_copied, 1)
                wait_alone(eng, id_copied, g + 1)
                gather_u(par, g, 0)
                if first:
                    gather_v(par, g, 0)
                    gather_u(par, g, 1)
                else:
                    gather_v(1 - par, g - 1, 1)
                    gather_u(par, g, 1)
                    gather_v(par, g, 0)

            eng.wait_ge(o_mm, 2 * BPH)
            head(0, 0, first=True)
            head(1, 1)
            with eng.Fori(1, NG // 2) as gg2:
                head(0, gg2 * 2)
                head(1, gg2 * 2 + 1)
            gather_v(1, NG - 1, 1)
            for s in range(RING):
                eng.wait_ge(v_in[s], 16 * 2 * NG)

        @block.scalar
        def _(eng):
            for s in (xa_ev, ga_ev, ri_ev, u_ev, g_a_ev, g_b_ev, out_ev):
                eng.sem_inc(s, 1)
            eng.sem_inc(q_ev, 2)

            def std(lo, hi, n):
                wait_alone(eng, var_ready, n)
                eng.activation(rstd[:, lo:hi], rstd[:, lo:hi], ACT.Sqrt).then_inc(std_ready, 1)

            def high_x(j):
                eng.wait_ge(xt_in[j], 16)
                eng.activation(x_parts[0][:, 2 * j:2 * j + 2, :], xt[:, 2 * j:2 * j + 2, :], ACT.Copy
                               ).then_inc(x_high, 1)

            def high_w(j, loads):
                wait_alone(eng, w_in[j], loads)
                eng.activation(w_parts[j][0][:, :], w_slot[j][:, 0:TILE], ACT.Copy).then_inc(w_high, 1)

            def a1_split():
                def gelus(half):
                    for n in range(BPH * half, BPH * half + BPH):
                        eng.wait_ge(v_mm, n + 1)
                        eng.activation(v_tok[:, n % BPH, half * HALF:(half + 1) * HALF],
                                       ps[:, TOKEN_BANKS[n], :], ACT.Gelu_apprx_tanh).then_inc(v_gelu, 1)

                for j in range(4):
                    high_x(j)
                    high_w(j, 16)
                for j in range(4):
                    eng.wait_ge(*((w_half_used, j + 1) if j < 3 else (v_mm, BPH)))
                    high_w(j, 32)
                eng.wait_ge(lam_abs, 1)
                eng.activation(sp[:, 1, :], sp[:, 0, :], ACT.Exp, scale=-1.0).then_inc(lam_exp, 1)
                gelus(0)
                for j in range(3):
                    eng.wait_ge(w_half_used, 3 + j + 1)
                    high_w(j, 48)
                gelus(1)
                std(0, BPH, 1)
                high_w(3, 48)
                high_w(4, 16)

            def a1(h, step):
                for n in A1_LATER[step]:
                    eng.wait_ge(v_mm, 2 * BPH * h + n + 1)
                    eng.activation(v_tok[:, n % BPH, (n // BPH) * HALF:(n // BPH + 1) * HALF],
                                   ps[:, V_BANK + n % 2, :], ACT.Gelu_apprx_tanh).then_inc(v_gelu, 1)
                if step == 5:
                    std(0, BPH, (BPH + 1) * h + 1)

            def high_y(i):
                lo, hi = Y_PIECES[i]
                eng.wait_ge(y_done, 1 + hi)
                eng.activation(y_parts[0][:, :, lo * P:hi * P], v_tok[:, :, lo * P:hi * P], ACT.Copy
                               ).then_inc(y_high, 1)

            def a2_step(h, c, step, ahead=0, y_first=False):
                n = c + (CT * h + 1)
                ch = lambda row: chan[:, row, bass.ds(c, 1)]
                def high_next(j):
                    if j < ahead:
                        high_w(j, c * 16 + (64 if j < 4 else 32))

                if step == 1:
                    wait_alone(eng, y_done, n)
                    wait_alone(eng, xa_mm, n)
                    eng.activation(xa[:, CONV - 1:], ps[:, XA, :], ACT.Copy).then_inc(xa_ev, 1)
                    high_next(0)
                    wait_alone(eng, ga_mm, n)
                    eng.activation(gg[:, :], ps[:, GA, :], ACT.Gelu_apprx_tanh).then_inc(ga_ev, 1)
                    high_next(1)
                    wait_alone(eng, mix_mm, n)
                    eng.wait_ge(v_norm, h + 1)
                    eng.activation(v_st[:, :, :], v_tok[:, :, bass.ds(c * P, P)], ACT.Copy
                                   ).then_inc(st_ready, 1)
                if step == 2:
                    wait_alone(eng, u_mm, n)
                    eng.activation(gu[:, :], ps[:, U, :], ACT.Gelu_apprx_tanh).then_inc(u_ev, 1)
                    high_next(2)
                    wait_alone(eng, ri_mm, n)
                    eng.activation(rr[:, :], ps[:, R, :], ACT.Sigmoid, bias=ch(BA))
                    eng.activation(ii[:, :], ps[:, I, :], ACT.Sigmoid, bias=ch(BX)).then_inc(ri_ev, 1)
                    eng.drain()
                    eng.activation(aa[:, :], rr[:, :], ACT.Exp, scale=dec[:, 0, bass.ds(c, 1)])
                    eng.drain()
                    eng.activation(rr[:, :], rr[:, :], ACT.Tanh, scale=dec[:, 1, bass.ds(c, 1)])
                    eng.activation(a2[:, :], aa[:, :], ACT.Square).then_inc(decay, 1)
                if step == 3:
                    wait_alone(eng, one_less, n)
                    eng.activation(rr[:, :], rr[:, :], ACT.Sqrt).then_inc(root, 1)
                    wait_alone(eng, g_a_mm, n)
                    eng.activation(s_a[:, :], ps[:, G_A, :], ACT.Sigmoid, bias=ch(BGA)).then_inc(g_a_ev, 1)
                    high_next(3)
                    wait_alone(eng, g_b_mm, n)
                    if y_first:
                        high_y(0)
                    eng.activation(s_b[:, :], ps[:, G_B, :], ACT.Sigmoid, bias=ch(BGB)).then_inc(g_b_ev, 1)
                    high_next(4)

            def a3_split():
                for i in range(1, len(Y_PIECES)):
                    high_y(i)
                for j in range(4):
                    eng.wait_ge(*((w_half_used, 6 + j + 1) if j < 3 else (o_mm, BPH)))
                    high_w(j, 16 * (2 + CT + 2))

            def copy_transposed(h, b):
                for j in range(2):
                    eng.wait_ge(t_mm, 2 * (BPH * h + b) + j + 1)
                    eng.activation(x1t[:, 4 * j:4 * j + 4, b * P:(b + 1) * P],
                                   ps[:, 2 + 4 * (b % 2) + j, :].rearrange("p (k t) -> p k t", k=4),
                                   ACT.Copy).then_inc(t_ev, 1)

            def a3(h, step):
                if step in (3, 4):
                    for b in (2 * step - 6, 2 * step - 5):
                        std(b, b + 1, (BPH + 1) * h + 2 + b)
                if step in (5, 6):
                    for b in (2 * step - 10, 2 * step - 9):
                        copy_transposed(h, b)

            def a4(h, step):
                t = step - 1
                if 0 <= t < QT:
                    eng.wait_ge(q_mm, QT * h + t + 1)
                    eng.wait_ge(sc_ev, QT * h + t + 1)
                    lo = first_block_of(h, t) * P
                    eng.activation(q_s[t % 2][:, lo:], ps[:, Q_BANK + t % 2, lo:], ACT.Copy).then_inc(q_ev, 1)

            def softmax_exp(g):
                wait_alone(eng, less_ready, g + 1)
                eng.activation(expo[:, :], less[:, :], ACT.Exp).then_inc(exp_done, 1)

            def gelu(g, c):
                wait_alone(eng, u_used, g * (2 * RING) + (RING * (c + 1) + RING))
                eng.activation(hact[:, c, :], hdot[:, c, :], ACT.Gelu_apprx_tanh).then_inc(gelu_done, 1)

            def load_next(b):
                eng.dma_start(x1_next[:, :], x1_d[bass.ds(b * P, P), :]).then_inc(next_in, 16)

            def store(b):
                wait_alone(eng, fin, b + 1)
                eng.dma_start(out[bass.ds(b * P, P), :], res[:, :]).then_inc(stored, 16)
                wait_alone(eng, stored, b * 16 + 16)

            def evacuate(b):
                wait_alone(eng, v_used, b * (HEADS * TOPK) + (HEADS * TOPK + RING))
                eng.activation(res[:, 0:HALF], ps[:, 0, :], ACT.Copy)
                eng.activation(res[:, HALF:D], ps[:, 1, :], ACT.Copy).then_inc(out_ev, 1)

            def final_std(b):
                wait_alone(eng, fin_var, b + 1)
                eng.activation(rstd2[:, :], rstd2[:, :], ACT.Sqrt).then_inc(fin_std, 1)

            def start_block(b, load=True):
                store(b - 2)
                evacuate(b - 1)
                if load:
                    wait_alone(eng, taken, b + 1)
                    load_next(b + 1)

            a1_split()
            eng.wait_ge(dec_ready, 1)
            with eng.Fori(0, CT - 1) as c:
                for s in range(4):
                    a2_step(0, c, s, ahead=5)
            for s in range(4):
                a2_step(0, CT - 1, s, ahead=4, y_first=True)
            a3_split()
            std(0, 1, 2)
            std(1, 2, 3)
            copy_transposed(0, 0)
            eng.wait_ge(first_q_mm, 1)
            eng.activation(first_q[:, :, :], ps[:, SC_BANK, 0:2 * P].rearrange("p (i t) -> p i t", i=2),
                           ACT.Copy).then_inc(first_q_ev, 1)
            softmax_exp(0)
            for b in (2, 3):
                std(b, b + 1, 2 + b)
            for b in (1, 2, 3):
                copy_transposed(0, b)
            eng.wait_ge(x1_stored, 16)
            load_next(1)

            def head(g, phase=None, step=0, chosen=True):
                for c in range(2):
                    gelu(g, c)
                    if phase is not None:
                        phase(step + c)
                    if chosen and c == 0:
                        softmax_exp(g + LEAD)

            def first_block(h):
                def phase(s):
                    if h:
                        a4(h, A4_AHEAD + s)
                    elif s < len(A4_FIRST_MM):
                        for t in A4_FIRST_MM[s]:
                            a4(h, t)
                    if h == 0 and s >= A1_FROM:
                        a1(1, s - A1_FROM)

                for k in range(HEADS):
                    head(BPH * HEADS * h + k, phase, 2 * k)

            def channel_tile(c):
                for k in range(2):
                    head(c * 2 + (HEADS + k), lambda s: a2_step(1, c, s), 2 * k)

            def last_block(s):
                if s < 8:
                    a3(1, s)
                elif s - 8 < A4_AHEAD:
                    a4(1, s - 8)

            first_block(0)
            evacuate(0)
            eng.wait_ge(taken, 2)
            load_next(2)
            eng.wait_ge(sc_ev, 2 + QT)
            with eng.Fori(0, 4) as c:
                channel_tile(c)
            final_std(0)
            start_block(2)
            with eng.Fori(4, 8) as c:
                channel_tile(c)
            final_std(1)
            start_block(3, load=False)
            for k in range(HEADS):
                head(24 + k, last_block, 2 * k)
                if k == 5:
                    eng.wait_ge(x1_stored, 32)
                    eng.wait_ge(taken, 4)
                    load_next(4)
            final_std(2)

            start_block(4)
            first_block(1)
            final_std(3)
            with eng.Fori(NBLK // 2 + 1, NBLK - 1) as b:
                start_block(b)
                with eng.Fori(0, HEADS) as hd:
                    head(b * HEADS + hd)
                final_std(b - 1)
            start_block(NBLK - 1, load=False)
            with eng.Fori(NG - HEADS, NG - LEAD) as g:
                head(g)
            with eng.Fori(NG - LEAD, NG) as g:
                head(g, chosen=False)
            final_std(NBLK - 2)
            store(NBLK - 2)
            evacuate(NBLK - 1)
            final_std(NBLK - 1)
            store(NBLK - 1)

        @block.tensor
        def _(eng):
            eng.sem_inc(v_used, RING)
            eng.sem_inc(mix_mm, 1)

            def project(bank, w, rhs, done, lo=0):
                for k in range(KT):
                    mm = eng.matmul(ps[:, bank, lo:], w[:, k, :], rhs[:, k, lo:],
                                    start=(k == 0), stop=(k == KT - 1))
                mm.then_inc(done, 1)

            def project_split(bank, j, done):
                for k in range(KT):
                    for a, b in PRODUCTS:
                        mm = eng.matmul(ps[:, bank, :], w_parts[j][a][:, k * P:(k + 1) * P], x_parts[b][:, k, :],
                                        start=(k == 0 and a + b == 0), stop=(k == KT - 1 and a == 1))
                mm.then_inc(done, 1)

            def a1_split():
                for half in range(2):
                    for k in range(KT):
                        j, col = k // 2, (k % 2) * HALF
                        if k % 2 == 0:
                            if half == 0:
                                eng.wait_ge(x_split, j + 1)
                            eng.wait_ge(w_split, 4 * half + j + 1)
                        for blk in range(BPH):
                            for a, b in PRODUCTS:
                                mm = eng.matmul(ps[:, TOKEN_BANKS[BPH * half + blk], :],
                                                x_parts[a][:, k, blk * P:(blk + 1) * P],
                                                w_parts[j][b][:, col:col + HALF],
                                                start=(k == 0 and a + b == 0), stop=(k == KT - 1 and a == 1))
                            if k == KT - 1:
                                mm.then_inc(v_mm, 1)
                        if k in (1, 3, 5):
                            mm.then_inc(w_half_used, 1)
                eng.wait_ge(v_gelu, BPH)

            def transpose(h, b):
                eng.wait_ge(x1_ready, BPH * h + b + 1)
                if b >= 2:
                    eng.wait_ge(t_ev, 2 * (BPH * h + b - 1))
                for j in range(2):
                    for k in range(4):
                        mm = eng.transpose(ps[:, 2 + 4 * (b % 2) + j, k * P:(k + 1) * P],
                                           x1[:, b, (4 * j + k) * P:(4 * j + k + 1) * P], ident[:, :])
                    mm.then_inc(t_mm, 1)

            def first_head():
                eng.wait_ge(t_ev, 2)
                for i in range(2):
                    eng.wait_ge(w_in[2 + i], 16 * (5 + CT))
                    for k in range(KT):
                        mm = eng.matmul(ps[:, SC_BANK, i * P:(i + 1) * P], wtile(2 + i)[:, k, :], x1t[:, k, 0:P],
                                        start=(k == 0), stop=(k == KT - 1))
                mm.then_inc(first_q_mm, 1)
                eng.wait_ge(first_q_ev, 1)
                for i in range(2):
                    mm = eng.matmul(ps[:, SC_BANK + 1, i * P:(i + 1) * P], first_q[:, i, :],
                                    w_slot[2 + i][:, TILE:QW], start=True, stop=True)
                mm.then_inc(first_sc_mm, 1)

            def a3_split():
                for free in (ri_ev, u_ev, g_a_ev, mix_ev, g_b_ev):
                    eng.wait_ge(free, CT + 1)
                def products(n, k):
                    half, blk = divmod(n, BPH)
                    j, col = k // 2, (k % 2) * HALF
                    for a, b in PRODUCTS:
                        mm = eng.matmul(ps[:, TOKEN_BANKS[n], :], y_parts[a][:, blk, k * P:(k + 1) * P],
                                        w_parts[j][b][:, col:col + HALF],
                                        start=(k == 0 and a + b == 0), stop=(k == KT - 1 and a == 1))
                    return mm

                for k in range(KT):
                    eng.wait_ge(y_split, next(i for i, (lo, hi) in enumerate(Y_PIECES) if k < hi) + 1)
                    if k % 2 == 0:
                        eng.wait_ge(w_split, A3_SPLIT + k // 2 + 1)
                    for n in range(BPH):
                        mm = products(n, k)
                        if k == KT - 1:
                            mm.then_inc(o_mm, 1)
                    if k in (1, 3, 5):
                        mm.then_inc(w_half_used, 1)
                for n in range(BPH, 2 * BPH):
                    if n == BPH + 2:
                        transpose(0, 0)
                    if n == BPH + 3:
                        first_head()
                    for k in range(KT):
                        if n == BPH and k % 2 == 0:
                            eng.wait_ge(w_split, A3_SPLIT + 4 + k // 2 + 1)
                        mm = products(n, k)
                    mm.then_inc(o_mm, 1)

            def token_rows(bank, lhs, b, n0, done, half=None):
                for k in range(KT):
                    if half is not None and k % 2 == 0:
                        eng.wait_ge(xt_in[k // 2], 16 * (half + 1))
                    if b == 0 and k % 2 == 0:
                        eng.wait_ge(w_in[k // 2], 16 * (n0 + 1))
                    mm = eng.matmul(ps[:, bank, :], lhs(k, b), wrow(k), start=(k == 0), stop=(k == KT - 1))
                mm.then_inc(done, 1)

            SLOT = 2 + CT + 2 + QT // 4

            def a1(h, step):
                for n in A1_STEPS[step]:
                    if n >= 2:
                        eng.wait_ge(v_gelu, 2 * BPH * h + n - 1)
                    token_rows(V_BANK + n % 2, lambda k, b: xt[:, k, b * P:(b + 1) * P], n % BPH,
                               SLOT * h + n // BPH, v_mm, half=h if n == 0 else None)
                if step == 5:
                    eng.wait_ge(v_gelu, 2 * BPH * (h + 1))

            def a2_step(h, c, step):
                n = c + (CT * h + 1)
                loaded = lambda j: eng.wait_ge(w_in[j], c * 16 + 16 * (SLOT * h + 3 if j < 4 else CT * h + 1))

                def mixed_in(bank, j, done):
                    if h == 0:
                        wait_alone(eng, w_split, c * 5 + (A2_SPLIT + j + 1))
                        project_split(bank, j, done)
                    else:
                        loaded(j)
                        project(bank, wtile(j), xt, done)

                if step == 0:
                    eng.wait_ge(ri_ev, n)
                    mixed_in(XA, 0, xa_mm)
                    mixed_in(GA, 1, ga_mm)
                if step == 1:
                    eng.wait_ge(u_ev, n)
                    mixed_in(U, 2, u_mm)
                    rg = w_slot[4][:, TILE:].rearrange("p (a c) -> p a c", a=2)
                    loaded(4)
                    eng.wait_ge(xc_ready, n)
                    eng.wait_ge(ga_ev, n + 1)
                    eng.matmul(ps[:, R, :], rg[:, 0, :], xc[:, :], start=True, stop=True)
                    eng.matmul(ps[:, I, :], rg[:, 1, :], xc[:, :], start=True, stop=True).then_inc(ri_mm, 1)
                if step == 2:
                    eng.wait_ge(g_a_ev, n)
                    mixed_in(G_A, 3, g_a_mm)
                    eng.wait_ge(st_ready, n)
                    eng.wait_ge(mix_ev, n)
                    for b in range(BPH):
                        mm = eng.matmul(ps[:, MIX, b * P:(b + 1) * P], v_st[:, b, :],
                                        ws[:, bass.ds(c, 1), :].rearrange("p a t -> p (a t)"),
                                        start=True, stop=True)
                    mm.then_inc(mix_mm, 1)
                    eng.wait_ge(g_b_ev, n)
                    mixed_in(G_B, 4, g_b_mm)

            def a3(h, step):
                if step == 0:
                    eng.wait_ge(y_done, CT * (h + 1) + 1)
                if step < 4:
                    for n in (2 * step, 2 * step + 1):
                        if n >= 2:
                            eng.wait_ge(o_ev, 2 * BPH * h + n - 1)
                        token_rows(O_BANK + n % 2, lambda k, b: v_tok[:, b, k * P:(k + 1) * P], n % BPH,
                                   SLOT * h + 2 + CT + n // BPH, o_mm)
                if step in (4, 5):
                    for b in (2 * step - 8, 2 * step - 7):
                        transpose(h, b)

            def a4(h, step):
                if step == 0:
                    eng.wait_ge(t_ev, 2 * BPH * (h + 1))
                t = step
                if t < QT:
                    eng.wait_ge(w_in[t % 4], 16 * (SLOT * h + 5 + CT + t // 4))
                    eng.wait_ge(q_ev, QT * h + t + 1)
                    project(Q_BANK + t % 2, wtile(t % 4), x1t, q_mm, lo=first_block_of(h, t) * P)
                t = step - 1
                if 0 <= t < QT:
                    eng.wait_ge(q_ev, QT * h + t + 3)
                    eng.wait_ge(sc_ev, QT * h + t + 1)
                    if h == 0 and t == 0:
                        eng.wait_ge(ids_ready, 1)
                    for b in range(first_block_of(h, t), BPH):
                        mm = eng.matmul(ps[:, SC_BANK + t % 2, b * P:(b + 1) * P],
                                        q_s[t % 2][:, b * P:(b + 1) * P], w_slot[t % 4][:, TILE:QW],
                                        start=True, stop=True)
                    mm.then_inc(sc_mm, 1)

            def seed(b):
                wait_alone(eng, taken, b + 1)
                eng.wait_ge(out_ev, b + 1)
                for j in range(2):
                    eng.matmul(ps[:, j, :], ident_a[:, :], x1_now[:, j * HALF:(j + 1) * HALF],
                               start=True, stop=True)

            def head(g, phase=None, step=0):
                for c in range(2):
                    if phase is not None:
                        phase(step + c)
                    for s in range(RING):
                        eng.wait_ge(diag_ready, g * (2 * RING) + (c * RING + s + 1))
                        eng.wait_ge(v_in[s], g * 32 + 16 * (c + 1))
                        for j in range(2):
                            mm = eng.matmul(ps[:, j, :], diag[:, s, :], v_ring[s][:, j * HALF:(j + 1) * HALF],
                                            start=False, stop=False, skip_group_check=True)
                        mm.then_inc(v_used, 1)

            a1_split()
            eng.wait_ge(masks, 1)
            with eng.Fori(0, CT) as c:
                for s in range(4):
                    a2_step(0, c, s)
            a3_split()
            for b in (1, 2, 3):
                transpose(0, b)

            def first_block(h):
                def phase(s):
                    if h:
                        a4(h, A4_AHEAD + s)
                    elif s < len(A4_FIRST_MM):
                        for t in A4_FIRST_MM[s]:
                            a4(h, t)
                    if h == 0 and s >= A1_FROM:
                        a1(1, s - A1_FROM)

                for k in range(HEADS):
                    head(BPH * HEADS * h + k, phase, 2 * k)

            def channel_tile(c):
                for k in range(2):
                    head(c * 2 + (HEADS + k), lambda s: a2_step(1, c, s), 2 * k)

            def last_block(s):
                if s < 8:
                    a3(1, s)
                elif s - 8 < A4_AHEAD:
                    a4(1, s - 8)

            seed(0)
            first_block(0)
            eng.wait_ge(sc_ev, 2 + QT)
            seed(1)
            with eng.Fori(0, 4) as c:
                channel_tile(c)
            seed(2)
            with eng.Fori(4, 8) as c:
                channel_tile(c)
            seed(3)
            for k in range(HEADS):
                head(24 + k, last_block, 2 * k)

            seed(4)
            first_block(1)
            with eng.Fori(NBLK // 2 + 1, NBLK) as b:
                seed(b)
                with eng.Fori(0, HEADS) as hd:
                    head(b * HEADS + hd)

        @block.vector
        def _(eng):
            eng.sem_inc(mix_ev, 1)
            eng.sem_inc(y_done, 1)
            eng.sem_inc(sc_ev, 2)
            eng.sem_inc(u_used, RING)
            eng.memset(halo[:, :, :], 0.0)
            eng.memset(h_last[:, :], 0.0)

            def variance(lo, hi):
                eng.drain()
                for b in range(lo, hi):
                    eng.bn_aggr(mv[:, b, :], stats[:, b, :, :])
                eng.drain()
                eng.tensor_scalar(rstd[:, lo:hi], mv[:, lo:hi, 1], EPS, None, ALU.add).then_inc(var_ready, 1)

            def inverse(lo, hi, n):
                eng.drain()
                eng.wait_ge(std_ready, n)
                eng.reciprocal(rstd[:, lo:hi], rstd[:, lo:hi])
                eng.drain()

            def normalise(data, mean, inv, gb):
                eng.scalar_tensor_tensor(out=data, in0=data, scalar=mean, in1=gb[:, 0, :],
                                         op0=ALU.subtract, op1=ALU.mult)
                eng.drain()
                return eng.scalar_tensor_tensor(out=data, in0=data, scalar=inv, in1=gb[:, 1, :],
                                                op0=ALU.mult, op1=ALU.add)

            def convolve(h, c):
                n = c + (CT * h + 1)
                ch = lambda row: chan[:, row, bass.ds(c, 1)]
                hal = halo[:, bass.ds(c, 1), :].rearrange("p a k -> p (a k)")
                eng.drain()
                eng.tensor_copy(xa[:, 0:CONV - 1], hal)
                eng.drain()
                eng.wait_ge(xa_ev, n + 1)
                eng.tensor_scalar(xc[:, :], xa[:, CONV - 1:], ch(CW + CONV - 1), ch(CB), ALU.mult, ALU.add)
                for k in range(CONV - 1):
                    eng.drain()
                    step = eng.scalar_tensor_tensor(out=xc[:, :], in0=xa[:, k:k + HALF], scalar=ch(CW + k),
                                                    in1=xc[:, :], op0=ALU.mult, op1=ALU.add)
                step.then_inc(xc_ready, 1)
                eng.tensor_copy(hal, xa[:, HALF:HALF + CONV - 1])

            def recur_and_merge(h, c, y_first=False):
                n = c + (CT * h + 1)
                eng.drain()
                eng.wait_ge(decay, n)
                eng.scalar_tensor_tensor(out=rr[:, :], in0=a2[:, :], scalar=1.0, in1=rr[:, :],
                                         op0=ALU.add, op1=ALU.mult).then_inc(one_less, 1)
                eng.tensor_tensor(ii[:, :], ii[:, :], xc[:, :], ALU.mult)
                eng.drain()
                eng.wait_ge(root, n)
                eng.tensor_tensor(ii[:, :], ii[:, :], rr[:, :], ALU.mult)
                eng.drain()
                eng.tensor_tensor_scan(a2[:, :], aa[:, :], ii[:, :], h_last[:, bass.ds(c, 1)],
                                       ALU.mult, ALU.add)
                eng.drain()
                eng.tensor_copy(h_last[:, bass.ds(c, 1)], a2[:, HALF - 1:HALF])
                eng.tensor_tensor(gg[:, :], gg[:, :], a2[:, :], ALU.mult)
                eng.drain()
                eng.wait_ge(g_a_ev, n + 1)
                eng.tensor_tensor(gg[:, :], gg[:, :], s_a[:, :], ALU.mult)
                eng.wait_ge(mix_mm, n + 1)
                bias = bs_b[:, bass.ds(c, 1), :].to_broadcast([P, BPH, P])
                eng.tensor_tensor(xc[:, :].rearrange("p (b t) -> p b t", b=BPH),
                                  ps[:, MIX, :].rearrange("p (b t) -> p b t", b=BPH), bias,
                                  ALU.add).then_inc(mix_ev, 1)
                eng.drain()
                eng.tensor_tensor(xc[:, :], xc[:, :], gu[:, :], ALU.mult)
                eng.drain()
                if y_first:
                    low_y(0)
                eng.wait_ge(g_b_ev, n + 1)
                eng.tensor_tensor(xc[:, :], xc[:, :], s_b[:, :], ALU.mult)
                eng.drain()
                eng.tensor_tensor(v_tok[:, :, bass.ds(c * P, P)],
                                  gg[:, :].rearrange("p (b t) -> p b t", b=BPH),
                                  xc[:, :].rearrange("p (b t) -> p b t", b=BPH), ALU.add).then_inc(y_done, 1)

            def best_keys(score, val, key, knocked):
                for sc, v in zip(score, val):
                    eng.max(v[:, 0:8], sc)
                eng.drain()
                for sc, v, kn in zip(score, val, knocked):
                    eng.match_replace(kn, v[:, 0:8], sc, LOWEST)
                for sc, v, k in zip(score, val, key):
                    eng.max_index(k[:, 0:8], v[:, 0:8], sc)
                eng.drain()
                for v, kn in zip(val, knocked):
                    eng.max(v[:, 8:16], kn)
                eng.drain()
                for v, k, kn in zip(val, key, knocked):
                    last = eng.max_index(k[:, 8:16], v[:, 8:16], kn)
                return last

            def top_keys(h, t):
                blocks = range(first_block_of(h, t), BPH)
                head_no, half_key = divmod(tile_of(h, t), 2)
                pair_no = [(BPH * h + b) * HEADS + head_no for b in blocks]
                eng.drain()
                eng.wait_ge(sc_mm, QT * h + t + 1)
                best_keys([ps[:, SC_BANK + t % 2, b * P:(b + 1) * P] for b in blocks],
                          [top_v[:, g, half_key, :] for g in pair_no],
                          [top_i[:, g, half_key, :] for g in pair_no],
                          [knock[:, b, :] for b in blocks]).then_inc(sc_ev, 1)

            def first_head():
                eng.drain()
                eng.wait_ge(first_sc_mm, 1)
                for i in range(2):
                    best_keys([ps[:, SC_BANK + 1, i * P:(i + 1) * P]], [top_v[:, 0, i, :]],
                              [top_i[:, 0, i, :]], [first_knock])
                    eng.drain()
                select(0)

            def low_x(j):
                quarter = slice(2 * j, 2 * j + 2)
                eng.wait_ge(x_high, j + 1)
                eng.tensor_tensor(x_parts[1][:, quarter, :], xt[:, quarter, :],
                                  x_parts[0][:, quarter, :].bitcast(F32), ALU.subtract).then_inc(x_split, 1)

            def low_w(j, tiles):
                wait_alone(eng, w_high, tiles)
                eng.tensor_tensor(w_parts[j][1][:, :], w_slot[j][:, 0:TILE],
                                  w_parts[j][0][:, :].bitcast(F32), ALU.subtract).then_inc(w_split, 1)

            def decay_rates():
                lam = chan[:, LAM, :]
                eng.wait_ge(const_in, 16 * 5)
                eng.tensor_scalar(sp[:, 5, :], lam, -1.0, None, ALU.mult)
                eng.drain()
                eng.tensor_tensor(sp[:, 0, :], lam, sp[:, 5, :], ALU.max).then_inc(lam_abs, 1)
                eng.wait_ge(lam_exp, 1)
                eng.tensor_scalar(sp[:, 2, :], sp[:, 1, :], 2.0, None, ALU.add)
                eng.drain()
                eng.reciprocal(sp[:, 2, :], sp[:, 2, :])
                eng.drain()
                eng.tensor_tensor(sp[:, 2, :], sp[:, 1, :], sp[:, 2, :], ALU.mult)
                eng.drain()
                eng.tensor_tensor(sp[:, 3, :], sp[:, 2, :], sp[:, 2, :], ALU.mult)
                terms = 9
                eng.drain()
                eng.tensor_scalar(sp[:, 4, :], sp[:, 3, :], 2.0 / (2 * terms + 1), 2.0 / (2 * terms - 1),
                                  ALU.mult, ALU.add)
                for k in range(terms - 2, -1, -1):
                    eng.drain()
                    eng.tensor_tensor(sp[:, 4, :], sp[:, 4, :], sp[:, 3, :], ALU.mult)
                    eng.drain()
                    eng.tensor_scalar(sp[:, 4, :], sp[:, 4, :], 2.0 / (2 * k + 1), None, ALU.add)
                eng.drain()
                eng.tensor_tensor(sp[:, 4, :], sp[:, 4, :], sp[:, 2, :], ALU.mult)
                eng.tensor_scalar(sp[:, 5, :], sp[:, 5, :], 0.0, None, ALU.max)
                eng.drain()
                eng.tensor_tensor(sp[:, 4, :], sp[:, 4, :], sp[:, 5, :], ALU.add)
                eng.drain()
                eng.tensor_scalar(dec[:, 0, :], sp[:, 4, :], -LRU_C, None, ALU.mult)
                eng.tensor_scalar(dec[:, 1, :], sp[:, 4, :], LRU_C, None, ALU.mult).then_inc(dec_ready, 1)
                eng.wait_ge(masks, 1)
                eng.tensor_scalar(ident_a[:, :], ident[:, :], ALPHA, None, ALU.mult)

            def a1_split():
                def statistics(half):
                    for b in range(BPH):
                        eng.wait_ge(v_gelu, BPH * half + b + 1)
                        eng.bn_stats(stats[:, b, half, :], v_tok[:, b, half * HALF:(half + 1) * HALF])

                for j in range(4):
                    low_x(j)
                    low_w(j, j + 1)
                eng.drain()
                for j in range(4):
                    low_w(j, 4 + j + 1)
                decay_rates()
                statistics(0)
                eng.drain()
                for j in range(3):
                    low_w(j, A2_SPLIT + j + 1)
                statistics(1)
                variance(0, BPH)
                low_w(3, A2_SPLIT + 4)
                low_w(4, A2_SPLIT + 5)
                inverse(0, BPH, 1)
                eng.wait_ge(ln_in, 32)
                normalise(v_tok[:, 0, :], mv[:, 0, 0:1], rstd[:, 0:1], ln_gb)
                convolve(0, 0)
                normalise_v(0, 1)

            def normalise_v(h, first=0):
                eng.wait_ge(ln_in, 32 * (2 * h + 1))
                for b in range(first, BPH):
                    last = normalise(v_tok[:, b, :], mv[:, b, 0:1], rstd[:, b:b + 1], ln_gb)
                last.then_inc(v_norm, 1)
                eng.drain()

            def a1(h, step):
                for n in A1_LATER[step]:
                    half, b = divmod(n, BPH)
                    eng.wait_ge(v_gelu, 2 * BPH * h + n + 1)
                    eng.bn_stats(stats[:, b, half, :], v_tok[:, b, half * HALF:(half + 1) * HALF])
                if step == 5:
                    variance(0, BPH)
                    inverse(0, BPH, (BPH + 1) * h + 1)
                    normalise_v(h)

            def low_y(i):
                lo, hi = Y_PIECES[i]
                eng.wait_ge(y_high, i + 1)
                eng.tensor_tensor(y_parts[1][:, :, lo * P:hi * P], v_tok[:, :, lo * P:hi * P],
                                  y_parts[0][:, :, lo * P:hi * P].bitcast(F32), ALU.subtract
                                  ).then_inc(y_split, 1)

            def a3_split():
                for i in range(1, len(Y_PIECES)):
                    low_y(i)
                for j in range(4):
                    low_w(j, A3_SPLIT + 4 + j + 1)

            def a2_step(h, c, step, ahead=0, convolved=False, y_first=False):
                def low_next(tiles):
                    for j in tiles:
                        if j < ahead:
                            low_w(j, c * 5 + (A2_SPLIT + 5 + j + 1))

                if step == 1:
                    if not convolved:
                        convolve(h, c)
                    low_next((0, 1, 2))
                if step == 3:
                    recur_and_merge(h, c, y_first)
                    low_next((3, 4))

            def a3(h, step):
                if step == 1:
                    eng.wait_ge(x_in, 16 * (h + 1))
                    eng.wait_ge(ln_in, 32 * (2 * h + 2))
                if 1 <= step <= 4:
                    for n in (2 * step - 2, 2 * step - 1):
                        half, b = divmod(n, BPH)
                        part = x1[:, b, half * HALF:(half + 1) * HALF]
                        bank = O_BANK + n % 2 if h else TOKEN_BANKS[n]
                        eng.wait_ge(o_mm, 2 * BPH * h + n + 1)
                        eng.scalar_tensor_tensor(out=part, in0=part, scalar=ALPHA, in1=ps[:, bank, :],
                                                 op0=ALU.mult, op1=ALU.add).then_inc(o_ev, 1)
                        eng.drain()
                        eng.bn_stats(stats[:, b, half, :], part)
                        if half:
                            variance(b, b + 1)
                            inverse(b, b + 1, (BPH + 1) * h + 2 + b)
                            normalise(x1[:, b, :], mv[:, b, 0:1], rstd[:, b:b + 1], ln_gb
                                      ).then_inc(x1_ready, 1)

            def a4(h, step):
                if 0 <= step - 2 < QT:
                    top_keys(h, step - 2)

            def select(g):
                val = top_v[:, bass.ds(g, 1), :, :].rearrange("p g a k -> p (g a) k")
                key = top_i[:, bass.ds(g, 1), :, :].rearrange("p g a k -> p (g a) k")
                grid = [P, TOPK, TOPK]
                eng.drain()
                eng.tensor_tensor(cand[:, :].rearrange("p (a b) -> p a b", a=TOPK),
                                  val[:, 0, :].unsqueeze(2).to_broadcast(grid),
                                  val[:, 1, :].unsqueeze(1).to_broadcast(grid), ALU.add)
                eng.drain()
                eng.max(best[:, 0:8], cand[:, :])
                eng.drain()
                eng.match_replace(cand2[:, :], best[:, 0:8], cand[:, :], LOWEST)
                eng.max_index(pos[:, 0:8], best[:, 0:8], cand[:, :])
                eng.drain()
                eng.max(best[:, 8:16], cand2[:, :])
                eng.drain()
                eng.max_index(pos[:, 8:16], best[:, 8:16], cand2[:, :])
                eng.tensor_scalar(less[:, :], best[:, :], best[:, 0:1], None, ALU.subtract
                                  ).then_inc(less_ready, 1)
                eng.drain()
                eng.tensor_scalar(pair[:, 0, :], pos[:, :], 4, None, ALU.logical_shift_right)
                eng.tensor_scalar(pair[:, 1, :], pos[:, :], TOPK - 1, None, ALU.bitwise_and)
                eng.drain()
                quad = [P, 2, TOPK, TOPK]
                eng.tensor_tensor(hot[:, :, :, :], pair[:, :, :].unsqueeze(3).to_broadcast(quad),
                                  iota[:, :].unsqueeze(1).unsqueeze(1).to_broadcast(quad), ALU.is_equal)
                eng.drain()
                eng.tensor_tensor(hot[:, :, :, :], hot[:, :, :, :],
                                  key.unsqueeze(2).to_broadcast(quad), ALU.mult)
                eng.drain()
                eng.tensor_reduce(picked[:, :, :], hot[:, :, :, :], AX_X, ALU.add)
                eng.drain()
                eng.scalar_tensor_tensor(out=ids[:, bass.ds(g, 1), :].rearrange("p g k -> p (g k)"),
                                         in0=picked[:, 0, :], scalar=float(NKEY), in1=picked[:, 1, :],
                                         op0=ALU.mult, op1=ALU.add).then_inc(ids_ready, 1)

            def gate(g):
                eng.drain()
                eng.wait_ge(exp_done, g + 1)
                eng.tensor_reduce(tot[:, 0:1], expo[:, :], AX_X, ALU.add)
                eng.drain()
                eng.reciprocal(tot[:, 1:2], tot[:, 0:1])
                eng.drain()
                eng.tensor_scalar(gates[:, bass.ds(g * TOPK, TOPK)], expo[:, :], tot[:, 1:2], None, ALU.mult)
                eng.drain()

            def dots(g, c):
                for s in range(RING):
                    eng.wait_ge(u_in[s], g * 32 + 16 * (c + 1))
                    eng.tensor_tensor_reduce(u_ring[s], u_ring[s], x1_now[:, :], 1.0, 0.0, ALU.mult, ALU.add,
                                             hdot[:, c, s:s + 1]).then_inc(u_used, 1)

            def diagonals(g, c):
                wait_alone(eng, gelu_done, g * 2 + (c + 1))
                eng.drain()
                eng.tensor_tensor(wact[:, :], hact[:, c, :], gates[:, bass.ds(g * TOPK + c * RING, RING)],
                                  ALU.mult)
                eng.drain()
                for s in range(RING):
                    eng.wait_ge(v_used, g * (2 * RING) + (c * RING + s + 1))
                    eng.tensor_scalar(diag[:, s, :], ident[:, :], wact[:, s:s + 1], None, ALU.mult
                                      ).then_inc(diag_ready, 1)

            def take_block(b):
                eng.drain()
                eng.wait_ge(next_in, b * 16)
                eng.tensor_copy(x1_now[:, :], x1_next[:, :]).then_inc(taken, 1)
                eng.drain()

            def finish(b):
                wait_alone(eng, out_ev, b + 2)
                eng.drain()
                for j in range(2):
                    eng.bn_stats(stats2[:, j, :], res[:, j * HALF:(j + 1) * HALF])
                eng.drain()
                eng.bn_aggr(mv2[:, :], stats2[:, :, :])
                eng.drain()
                eng.tensor_scalar(rstd2[:, :], mv2[:, 1:2], EPS, None, ALU.add).then_inc(fin_var, 1)
                eng.drain()
                eng.wait_ge(fin_std, b + 1)
                eng.reciprocal(rstd2[:, :], rstd2[:, :])
                eng.drain()
                normalise(res[:, :], mv2[:, 0:1], rstd2[:, 0:1], ln2_gb).then_inc(fin, 1)

            a1_split()
            for s in range(4):
                a2_step(0, 0, s, ahead=5, convolved=True)
            with eng.Fori(1, CT - 1) as c:
                for s in range(4):
                    a2_step(0, c, s, ahead=5)
            for s in range(4):
                a2_step(0, CT - 1, s, ahead=4, y_first=True)
            a3_split()
            for s in range(4):
                a3(0, s)
            first_head()
            a3(0, 4)
            eng.drain()
            eng.tensor_copy(x1_now[:, :], x1[:, 0, :]).then_inc(taken, 1)
            gate(0)

            def head(g, phase=None, step=0, chosen=True, first=False):
                dots(g, 0)
                if not first:
                    diagonals(g - 1, 1)
                if phase is not None:
                    phase(step)
                if chosen:
                    select(g + LEAD)
                dots(g, 1)
                diagonals(g, 0)
                if phase is not None:
                    phase(step + 1)
                if chosen:
                    gate(g + LEAD)

            def first_block(h):
                def phase(s):
                    if h:
                        a4(h, A4_AHEAD + s)
                    elif s < len(A4_FIRST):
                        for t in A4_FIRST[s]:
                            a4(h, t)
                    if h == 0 and s >= A1_FROM:
                        a1(1, s - A1_FROM)

                for k in range(HEADS):
                    head(BPH * HEADS * h + k, phase, 2 * k, first=(h == 0 and k == 0))

            def channel_tile(c):
                for k in range(2):
                    head(c * 2 + (HEADS + k), lambda s: a2_step(1, c, s), 2 * k)

            def last_block(s):
                if s < 8:
                    a3(1, s)
                elif s - 8 < A4_AHEAD:
                    a4(1, s - 8)

            first_block(0)
            take_block(1)
            with eng.Fori(0, 4) as c:
                channel_tile(c)
            finish(0)
            take_block(2)
            with eng.Fori(4, 8) as c:
                channel_tile(c)
            finish(1)
            take_block(3)
            for k in range(HEADS):
                head(24 + k, last_block, 2 * k)
            finish(2)

            take_block(4)
            first_block(1)
            finish(3)
            with eng.Fori(NBLK // 2 + 1, NBLK - 1) as b:
                take_block(b)
                with eng.Fori(0, HEADS) as hd:
                    head(b * HEADS + hd)
                finish(b - 1)
            take_block(NBLK - 1)
            with eng.Fori(NG - HEADS, NG - LEAD) as g:
                head(g)
            with eng.Fori(NG - LEAD, NG) as g:
                head(g, chosen=False)
            diagonals(NG - 1, 1)
            finish(NBLK - 2)
            finish(NBLK - 1)


def kernel(**inputs):
    import numpy as np
    import concourse.bacc as bacc
    from concourse.bass_utils import run_bass_kernel_spmd

    a = {k: np.asarray(v) for k, v in inputs.items()}

    def tiles(w):
        return w.reshape(KT, P, -1, P).transpose(2, 1, 0, 3)

    def halves(w):
        return w.reshape(KT, P, 2, HALF).transpose(2, 1, 0, 3).reshape(2, P, KT * HALF)

    w_in = a["w_in"][0]
    wt = tiles(w_in)
    mix = [wt[CT * j:CT * (j + 1)].reshape(CT, P, TILE) for j in (0, 1, 2, 4, 5)]
    keys_t = a["peer_sub_keys"][0].reshape(QT, NKEY, P).transpose(0, 2, 1)
    cols = np.concatenate([a["conv_w"][0], a["conv_b"], a["rg_b_a"], a["rg_b_x"], a["rg_lambda"],
                           a["b_gate"][0]])
    arrays = {
        "x": a["x"][0],
        "x_t": a["x"][0].T.reshape(KT, P, NHALF, HALF).transpose(2, 1, 0, 3).reshape(NHALF, P, KT * HALF),
        "w_mix": np.stack(mix[:4]),
        "w_gb": np.concatenate([mix[4], a["rg_w_a"][0], a["rg_w_x"][0]], axis=2),
        "w_v": halves(w_in[:, 3 * D:4 * D]),
        "w_out": halves(a["w_out"][0]),
        "w_q": np.concatenate([tiles(a["peer_wq"][0]).reshape(QT, P, TILE), keys_t], axis=2),
        "ws_t": a["gm_ws"][0].transpose(2, 0, 1),
        "bs": a["gm_bs"][0].reshape(-1),
        "chan": cols.reshape(NCHAN, CT, P).transpose(2, 0, 1),
        "ln": np.stack([np.stack([a[g][0], a[b][0]]) for g, b in
                        (("gm_ln_g", "gm_ln_b"), ("ln1_g", "ln1_b"), ("ln2_g", "ln2_b"))]),
        "peer_u": a["peer_u"][0],
        "peer_v": a["peer_v"][0],
    }
    arrays = {f"{k}_dram": np.ascontiguousarray(v) for k, v in arrays.items()}
    nc = bacc.Bacc("TRN2", target_bir_lowering=False, num_devices=1)
    args = [nc.dram_tensor(k, v.shape, mybir.dt.from_np(v.dtype), kind="ExternalInput").ap()
            for k, v in arrays.items()]
    out = nc.dram_tensor("out_dram", (T, D), F32, kind="ExternalOutput").ap()
    x1_d = nc.dram_tensor("x1_scratch", (T, D), F32, kind="Internal").ap()
    build(nc, *args, x1_d, out)
    r = run_bass_kernel_spmd(nc, [arrays], core_ids=[0])
    return r.results[0]["out_dram"].reshape(1, T, D)
```
